# Optimizing a Trainium2 kernel written in Bass

```python
import jax, jax.numpy as jnp
from jax import lax
import numpy as np

D_MODEL = 1024
BATCH = 1
SEQ = 2048
DEPTH = 1
DEC_BATCH = 8
DEC_SEQ = 4
PAST_LEN = 16384
PAGE_SIZE = 128

MIX_W = D_MODEL
H_GLA = 4
DV_GLA = MIX_W // 2 // H_GLA
DK_GLA = DV_GLA // 2
GLA_RANK = 16
GLA_TAU = 16.0
H_GDN = 4
DK_GDN = MIX_W // 2 // H_GDN
DV_GDN = DK_GDN
GDN_CONV_W = 4
D_FF = ((8 * D_MODEL // 3) + 127) // 128 * 128
FFN_CONV_W = 3
CHUNK = 32
EPS = 1e-6

GLA_QK = H_GLA * DK_GLA
GLA_V = H_GLA * DV_GLA
GDN_QK = H_GDN * DK_GDN
GDN_V = H_GDN * DV_GDN
GDN_CONV_C = 2 * GDN_QK + GDN_V
IN_SIZES = [GLA_QK, GLA_QK, GLA_V, GLA_V, GLA_RANK, GDN_CONV_C, GDN_V, H_GDN, H_GDN]
N_IN = sum(IN_SIZES)
IN_IDX = list(np.cumsum(IN_SIZES)[:-1].tolist())

kernel_name = "hymba_gla_gdn_convffn_step"

def rmsnorm(x, g):
    xf = x.astype(jnp.float32)
    y = xf * lax.rsqrt(jnp.mean(xf * xf, axis=-1, keepdims=True) + EPS) * g.astype(jnp.float32)
    return y.astype(x.dtype)

def l2norm(x):
    xf = x.astype(jnp.float32)
    return xf * lax.rsqrt(jnp.sum(xf * xf, axis=-1, keepdims=True) + EPS)

def causal_dwconv(x, buf, w):
    W = w.shape[0]
    C = x.shape[-1]
    xc = jnp.concatenate([buf.astype(x.dtype), x], axis=1)
    y = lax.conv_general_dilated(xc, w[:, None, :].astype(x.dtype), (1,), 'VALID',
                                 dimension_numbers=('NWC', 'WIO', 'NWC'),
                                 feature_group_count=C)
    return y, xc[:, xc.shape[1] - (W - 1):]

def to_chunks(a):
    B, T = a.shape[0], a.shape[1]
    pad = (-T) % CHUNK
    a = jnp.pad(a, [(0, 0), (0, pad)] + [(0, 0)] * (a.ndim - 2))
    nc = (T + pad) // CHUNK
    a = a.reshape((B, nc, CHUNK) + a.shape[2:])
    perm = (1, 0, 3, 2) + tuple(range(4, a.ndim))
    return a.transpose(perm)

def from_chunks(o, T):
    nc, B, H, C, dv = o.shape
    return o.transpose(1, 0, 3, 2, 4).reshape(B, nc * C, H, dv)[:, :T]

def gla_chunked(q, k, v, log_a, h0):
    T = q.shape[1]
    f32 = jnp.float32
    qc, kc, vc, ac = (to_chunks(t.astype(f32)) for t in (q, k, v, log_a))
    incl = jnp.tril(jnp.ones((CHUNK, CHUNK), bool))

    def step(h, inp):
        qi, ki, vi, ai = inp
        b = jnp.cumsum(ai, axis=-2)
        diff = b[..., :, None, :] - b[..., None, :, :]
        decay = jnp.exp(jnp.where(incl[:, :, None], diff, -jnp.inf))
        attn = jnp.einsum('bhid,bhjd,bhijd->bhij', qi, ki, decay)
        o = (jnp.einsum('bhij,bhjv->bhiv', attn, vi)
             + jnp.einsum('bhid,bhdv->bhiv', qi * jnp.exp(b), h))
        b_last = b[..., -1:, :]
        h_new = (jnp.exp(b_last)[..., 0, :, None] * h
                 + jnp.einsum('bhjd,bhjv->bhdv', ki * jnp.exp(b_last - b), vi))
        return h_new, o

    h_fin, o = lax.scan(step, h0.astype(f32), (qc, kc, vc, ac))
    return from_chunks(o, T), h_fin

def gdn_chunked(q, k, v, g, beta, h0):
    T = q.shape[1]
    f32 = jnp.float32
    qc, kc, vc, gc, bc = (to_chunks(t.astype(f32)) for t in (q, k, v, g, beta))
    incl = jnp.tril(jnp.ones((CHUNK, CHUNK), bool))
    strict = jnp.tril(jnp.ones((CHUNK, CHUNK), bool), -1)
    eye = jnp.eye(CHUNK, dtype=f32)

    def step(h, inp):
        qi, ki, vi, gi, bi = inp
        G = jnp.cumsum(gi, axis=-1)
        diff = G[..., :, None] - G[..., None, :]
        decay = jnp.exp(jnp.where(incl, diff, -jnp.inf))
        kk = jnp.einsum('bhid,bhjd->bhij', ki, ki)
        L = jnp.where(strict, bi[..., :, None] * kk * decay, 0.0)
        eG = jnp.exp(G)[..., None]
        rhs = bi[..., None] * (vi - eG * jnp.einsum('bhid,bhdv->bhiv', ki, h))
        U = lax.linalg.triangular_solve(L + eye, rhs, left_side=True, lower=True,
                                        unit_diagonal=True)
        qk = jnp.einsum('bhid,bhjd->bhij', qi, ki) * decay
        o = eG * jnp.einsum('bhid,bhdv->bhiv', qi, h) + jnp.einsum('bhij,bhjv->bhiv', qk, U)
        G_last = G[..., -1:]
        h_new = (jnp.exp(G_last)[..., None] * h
                 + jnp.einsum('bhjd,bhjv->bhdv', ki * jnp.exp(G_last - G)[..., None], U))
        return h_new, o

    h_fin, o = lax.scan(step, h0.astype(f32), (qc, kc, vc, gc, bc))
    return from_chunks(o, T), h_fin

def trunk(x, st_gla, st_gdn, st_conv, st_ffn, params):
    (norm1_g, w_in, gla_w_a2, gla_b_a, gla_norm_g, gdn_conv_w, gdn_a_log, gdn_dt_bias,
     gdn_norm_g, w_out, norm2_g, w_up, ffn_conv_w, w_down, norm_f_g) = params
    B, T = x.shape[0], x.shape[1]
    dt = x.dtype
    n_gla, n_gdn, n_conv, n_ffn = [], [], [], []
    for l in range(DEPTH):
        hn = rmsnorm(x, norm1_g[l])
        proj = hn @ w_in[l]
        q_a, k_a, v_a, gate_a, low_a, qkv_b, z_b, beta_b, dec_b = jnp.split(proj, IN_IDX, axis=-1)
        q = q_a.reshape(B, T, H_GLA, DK_GLA) * (DK_GLA ** -0.5)
        k = k_a.reshape(B, T, H_GLA, DK_GLA)
        v = v_a.reshape(B, T, H_GLA, DV_GLA)
        log_a = jax.nn.log_sigmoid((low_a @ gla_w_a2[l] + gla_b_a[l]).astype(jnp.float32)) / GLA_TAU
        o_a, h_a = gla_chunked(q, k, v, log_a.reshape(B, T, H_GLA, DK_GLA), st_gla[l])
        o_a = rmsnorm(o_a.astype(dt), gla_norm_g[l]) * jax.nn.silu(gate_a.reshape(B, T, H_GLA, DV_GLA))
        qkv, conv_new = causal_dwconv(qkv_b, st_conv[l], gdn_conv_w[l])
        qkv = jax.nn.silu(qkv)
        qd, kd, vd = jnp.split(qkv, [GDN_QK, 2 * GDN_QK], axis=-1)
        qd = l2norm(qd.reshape(B, T, H_GDN, DK_GDN)) * (DK_GDN ** -0.5)
        kd = l2norm(kd.reshape(B, T, H_GDN, DK_GDN))
        vd = vd.reshape(B, T, H_GDN, DV_GDN)
        g = -jnp.exp(gdn_a_log[l].astype(jnp.float32)) * jax.nn.softplus(
            dec_b.astype(jnp.float32) + gdn_dt_bias[l].astype(jnp.float32))
        beta = jax.nn.sigmoid(beta_b.astype(jnp.float32))
        o_b, h_b = gdn_chunked(qd, kd, vd, g, beta, st_gdn[l])
        o_b = rmsnorm(o_b.astype(dt), gdn_norm_g[l]) * jax.nn.silu(z_b.reshape(B, T, H_GDN, DV_GDN))
        mix = jnp.concatenate([o_a.reshape(B, T, GLA_V), o_b.reshape(B, T, GDN_V)], axis=-1)
        x = x + mix @ w_out[l]
        hn2 = rmsnorm(x, norm2_g[l])
        up, ffn_new = causal_dwconv(hn2 @ w_up[l], st_ffn[l], ffn_conv_w[l])
        a_f, b_f = jnp.split(up, [D_FF], axis=-1)
        x = x + (jax.nn.silu(a_f) * b_f) @ w_down[l]
        n_gla.append(h_a.astype(st_gla.dtype))
        n_gdn.append(h_b.astype(st_gdn.dtype))
        n_conv.append(conv_new.astype(st_conv.dtype))
        n_ffn.append(ffn_new.astype(st_ffn.dtype))
    y = rmsnorm(x, norm_f_g)
    return y, jnp.stack(n_gla), jnp.stack(n_gdn), jnp.stack(n_conv), jnp.stack(n_ffn)

def setup_inputs(seed: int = 0) -> dict:
    key = jax.random.key(seed)
    ks = jax.random.split(key, 24)
    nrm = jax.random.normal
    f32 = jnp.float32
    dt_min, dt_max = 0.001, 0.1
    dt0 = jnp.exp(jax.random.uniform(ks[13], (DEPTH, H_GDN), f32) * (np.log(dt_max) - np.log(dt_min)) + np.log(dt_min))
    return {
        "x_prompt": nrm(ks[0], (BATCH, SEQ, D_MODEL), f32),
        "x_sample": nrm(ks[1], (DEC_BATCH, DEC_SEQ, D_MODEL), f32),
        "state_gla": 0.3 * nrm(ks[2], (DEPTH, DEC_BATCH, H_GLA, DK_GLA, DV_GLA), f32),
        "state_gdn": 0.1 * nrm(ks[3], (DEPTH, DEC_BATCH, H_GDN, DK_GDN, DV_GDN), f32),
        "state_gdn_conv": nrm(ks[4], (DEPTH, DEC_BATCH, GDN_CONV_W - 1, GDN_CONV_C), f32),
        "state_ffn_conv": nrm(ks[5], (DEPTH, DEC_BATCH, FFN_CONV_W - 1, 2 * D_FF), f32),
        "norm1_g": 1.0 + 0.02 * nrm(ks[6], (DEPTH, D_MODEL), f32),
        "w_in": nrm(ks[7], (DEPTH, D_MODEL, N_IN), f32) * D_MODEL ** -0.5,
        "gla_w_a2": nrm(ks[8], (DEPTH, GLA_RANK, GLA_QK), f32) * GLA_RANK ** -0.5,
        "gla_b_a": 0.1 * nrm(ks[9], (DEPTH, GLA_QK), f32),
        "gla_norm_g": 1.0 + 0.02 * nrm(ks[10], (DEPTH, DV_GLA), f32),
        "gdn_conv_w": nrm(ks[11], (DEPTH, GDN_CONV_W, GDN_CONV_C), f32) * GDN_CONV_W ** -0.5,
        "gdn_a_log": jnp.log(jax.random.uniform(ks[12], (DEPTH, H_GDN), f32, 1.0, 16.0)),
        "gdn_dt_bias": dt0 + jnp.log(-jnp.expm1(-dt0)),
        "gdn_norm_g": 1.0 + 0.02 * nrm(ks[14], (DEPTH, DV_GDN), f32),
        "w_out": nrm(ks[15], (DEPTH, MIX_W, D_MODEL), f32) * MIX_W ** -0.5,
        "norm2_g": 1.0 + 0.02 * nrm(ks[16], (DEPTH, D_MODEL), f32),
        "w_up": nrm(ks[17], (DEPTH, D_MODEL, 2 * D_FF), f32) * D_MODEL ** -0.5,
        "ffn_conv_w": nrm(ks[18], (DEPTH, FFN_CONV_W, 2 * D_FF), f32) * FFN_CONV_W ** -0.5,
        "w_down": nrm(ks[19], (DEPTH, D_FF, D_MODEL), f32) * D_FF ** -0.5,
        "norm_f_g": 1.0 + 0.02 * nrm(ks[20], (D_MODEL,), f32),
    }

def reference(x_prompt, x_sample, state_gla, state_gdn, state_gdn_conv, state_ffn_conv,
              norm1_g, w_in, gla_w_a2, gla_b_a, gla_norm_g, gdn_conv_w, gdn_a_log, gdn_dt_bias,
              gdn_norm_g, w_out, norm2_g, w_up, ffn_conv_w, w_down, norm_f_g):
    params = (norm1_g, w_in, gla_w_a2, gla_b_a, gla_norm_g, gdn_conv_w, gdn_a_log, gdn_dt_bias,
              gdn_norm_g, w_out, norm2_g, w_up, ffn_conv_w, w_down, norm_f_g)
    Bp = x_prompt.shape[0]
    dt = x_prompt.dtype
    z_gla = jnp.zeros((DEPTH, Bp) + state_gla.shape[2:], state_gla.dtype)
    z_gdn = jnp.zeros((DEPTH, Bp) + state_gdn.shape[2:], state_gdn.dtype)
    z_conv = jnp.zeros((DEPTH, Bp) + state_gdn_conv.shape[2:], dt)
    z_ffn = jnp.zeros((DEPTH, Bp) + state_ffn_conv.shape[2:], dt)
    y_prompt, p_gla, p_gdn, p_conv, p_ffn = trunk(x_prompt, z_gla, z_gdn, z_conv, z_ffn, params)
    y_sample, s_gla, s_gdn, s_conv, s_ffn = trunk(x_sample, state_gla, state_gdn, state_gdn_conv,
                                                  state_ffn_conv, params)
    return (y_prompt, y_sample, p_gla, p_gdn, p_conv, p_ffn, s_gla, s_gdn, s_conv, s_ffn)


_drawn_inputs = setup_inputs


def setup_inputs(seed=0):
    import zlib

    import numpy as np

    out = dict(_drawn_inputs(seed))
    spreads = {}
    factors = {'gla_norm_g': 6.229, 'gdn_norm_g': 7.196, 'norm2_g': 2.864, 'norm_f_g': 2.95}
    for name, (base, spread) in spreads.items():
        noise = np.random.default_rng([zlib.crc32(name.encode()), seed]).standard_normal(out[name].shape)
        drawn = base * np.exp(spread * noise) if base else spread * noise
        out[name] = __import__('jax').numpy.asarray(drawn.astype(out[name].dtype))
    for name, factor in factors.items():
        out[name] = (out[name] * factor).astype(out[name].dtype)
    return out
```

```python
import math
from contextlib import ExitStack

import concourse.bass as bass
from concourse import mybir

F32 = mybir.dt.float32
I32 = mybir.dt.int32
ALU = mybir.AluOpType
ACT = mybir.ActivationFunctionType
AX_X = mybir.AxisListType.X

D = 1024
T = 2048
NB, TS = 8, 4
S = NB * TS
C = 128
TILES = T // C
KT = D // C
H = 4
DKA, DV = 64, 128
RANK = 16
QKV = 3 * H * DV
CT = QKV // C
NIN = 3608
GROUPS = 8
PARTS = 4 * GROUPS
GW = NIN // GROUPS
O_QA, O_VA, O_GA, O_LOW, O_QKV, O_Z, O_BETA, O_DEC = 0, 512, 1024, 1536, 1552, 3088, 3600, 3604
EPS = 1e-6
ABS_BITS = 0x7FFFFFFF
SPANS = [64, 32, 16, 8, 4, 2, 1]
NL = len(SPANS)
SAMPLE_LEVELS = [NL - 2, NL - 1]
E_LAST, E_ZERO = NL, NL + 1
NE = NL + 2
ROUNDS = (NL + 1) // 2

DFF = 2816
FT = DFF // C
ALL = T + S
UB = 5
UW = ALL // UB
YT = TILES + 1


def mixers(nc, x_prompt, x_sample, state_gla, state_gdn, state_conv, norm1_g, w_in, w_a2, b_a,
           gla_g, conv_w, a_log, dt_bias, gdn_g, mix_t,
           gla_p, gdn_p, conv_p, gla_s, gdn_s, conv_s):
    with ExitStack() as ctx:
        def sb(name, shape, dt=F32):
            return ctx.enter_context(nc.sbuf_tensor(name, shape, dt))

        bank = [ctx.enter_context(nc.psum_tensor(f"mixer_bank{i}", [C, 512], F32)) for i in range(8)]

        w = sb("w_in_sb", [C, KT, NIN])
        ident = sb("ident", [C, C])
        ones = sb("ones", [C, C])
        level = sb("level", [C, NL, C])
        incl = sb("incl", [C, C])
        incl_s = sb("incl_s", [S, S])
        seq_s = sb("seq_s", [S, S])
        cols_s = sb("cols_s", [C, NB, S])
        rows_s = sb("rows_s", [S, NB])
        reset_s = sb("reset_s", [C, S])
        g1 = sb("g1", [C, KT])
        wa2 = sb("wa2", [RANK, 2 * C])
        ba = sb("ba", [C, 2])
        gains = sb("gains", [C, 2, DV])
        alog = sb("alog", [C, H])
        dtb = sb("dtb", [C, H])
        expa = sb("expa", [C, H])
        cw = sb("cw", [C, CT, 28])
        one, eps, eps4, lnq, spare = (sb(x, [C, 1]) for x in ("one", "eps", "eps4", "lnq", "spare"))
        xt = sb("xt", [C, D])
        xn = sb("xn", [C, D])
        x_ss = sb("x_ss", [C, 1])
        x_ln = sb("x_ln", [C, 1])
        x_rs = sb("x_rs", [C, 1])
        hnt = sb("hnt", [C, KT, C])
        proj = sb("proj", [C, NIN])
        qka = sb("qka", [C, 4, C])
        va = sb("va", [C, H, DV])
        lowt = sb("lowt", [RANK, C])
        bcum = sb("bcum", [C, 2, C])
        ex = sb("ex", [C, NE, 2, C])
        ke = ex
        qe = sb("qe", [C, NL, 2, C])
        la_abs, la_exp, la_ln, la_min, la = (qe[:, i] for i in range(5))
        q0 = sb("q0", [C, 2, C])
        kl = ex[:, E_LAST]
        ked = sb("ked", [C, 2 * C])
        at = sb("at", [C, 2, 2, C])
        hgla = sb("hgla", [C, H, DV])
        gate = sb("gate", [C, 2, H, DV])
        tbeta, dabs, dexp, dln, drel, gg, gcol, gend, nbeta, hbeta, egcol, begcol, gdist, gdec = (
            sb(x, [C, H]) for x in ("tbeta dabs dexp dln drel gg gcol gend nbeta hbeta egcol begcol "
                                    "gdist gdec").split())
        cx = sb("cx", [C, CT, 3 + C])
        cv = sb("cv", [C, CT, C])
        th = sb("th", [C, CT, C])
        egrow = sb("egrow", [C, H, C])
        dtt = sb("dtt", [C, H, C])
        lt = dtt
        ug = sb("ug", [C, H, C])
        dti = ug
        ab = ug

        def shared(v, i):
            return v[:, 512 * i:512 * i + 512].rearrange("p (h i) -> p h i", h=H)
        qe_, ex_, th_ = (v[:].rearrange("p l g i -> p (l g i)") if v is not th else
                         v[:].rearrange("p c i -> p (c i)") for v in (qe, ex, th))
        xi, xit, pp = (shared(qe_, i) for i in range(3))
        ltm = shared(ex_, 0)
        wt = shared(ex_, 1)
        uu = shared(ex_, 2)
        kb, kh, vb = (shared(th_, i) for i in range(3))
        hgdn = sb("hgdn", [C, H, DV])
        osq = [cv[:, 8:12, :], kb]
        o_ss = sb("o_ss", [C, 2, H])
        o_lnm = sb("o_lnm", [C, 2, H])
        o_rs = sb("o_rs", [C, 2, H])
        mixt = qe_[:, 0:2 * H * C].rearrange("p (h i) -> p h i", h=2 * H)

        free = w[:, :, :].rearrange("p k n -> p (k n)")

        def after_w(at_, n, *dims):
            v = free[:, at_:at_ + n]
            names = " ".join("abc"[:len(dims)])
            return v.rearrange(f"p ({names}) -> p {names}", **dict(zip("abc", dims)))
        hs_gla = after_w(0, H * NB * DV, H, NB, DV)
        hs_gdn = after_w(4096, H * NB * DV, H, NB, DV)
        mq_gla = after_w(8192, 2 * NB * S, 2, NB, S)
        mq_gdn = after_w(8704, H * NB * S, H, NB, S)
        mw_gdn = after_w(9728, H * NB * S, H, NB, S)
        mk_gla = after_w(10752, NB * 2 * C, NB, 2 * C)
        mk_gdn = after_w(12800, NB * H * DV, NB, H, DV)

        def sem(name):
            return ctx.enter_context(nc.semaphore(name))

        s_w_loaded = sem("w_loaded")
        s_consts_loaded = sem("consts_loaded")
        s_taps_loaded = sem("taps_loaded")
        s_x_loaded = sem("x_loaded")
        s_masks_made = sem("masks_made")
        s_cw_turned = sem("cw_turned")
        s_cw_out = sem("cw_out")
        s_expa_made = sem("expa_made")
        s_x_squared = sem("x_squared")
        s_x_lned = sem("x_lned")
        s_x_rsed = sem("x_rsed")
        s_x_normed = sem("x_normed")
        s_hn_turned = sem("hn_turned")
        s_hn_out = sem("hn_out")
        s_proj_done = sem("proj_done")
        s_proj_out = sem("proj_out")
        s_turned = sem("turned")
        s_qka_out = sem("qka_out")
        s_cx_out = sem("cx_out")
        s_low_out = sem("low_out")
        s_va_copied = sem("va_copied")
        s_gates_tanh = sem("gates_tanh")
        s_gates_silu = sem("gates_silu")
        s_gates_made = sem("gates_made")
        s_tap = sem("tap")
        s_halo_kept = sem("halo_kept")
        s_conv_tanh = sem("conv_tanh")
        s_conv_silu = sem("conv_silu")
        s_conv_sq = sem("conv_sq")
        s_sums_done = sem("sums_done")
        s_norm_ln = sem("norm_ln")
        s_norm_rs = sem("norm_rs")
        s_qk_normed = sem("qk_normed")
        s_a_done = sem("a_done")
        s_a_abs = sem("a_abs")
        s_a_exp = sem("a_exp")
        s_a_ln = sem("a_ln")
        s_a_min = sem("a_min")
        s_la_made = sem("la_made")
        s_b_made = sem("b_made")
        s_dist_made = sem("dist_made")
        s_dist_abs = sem("dist_abs")
        s_ex_made = sem("ex_made")
        s_qe_made = sem("qe_made")
        s_ke_made = sem("ke_made")
        s_at_done = sem("at_done")
        s_at_level = sem("at_level")
        s_kl_turned = sem("kl_turned")
        s_ked_out = sem("ked_out")
        s_d_abs = sem("d_abs")
        s_d_exp = sem("d_exp")
        s_d_ln = sem("d_ln")
        s_d_rel = sem("d_rel")
        s_d_sum = sem("d_sum")
        s_g_made = sem("g_made")
        s_gcum_done = sem("gcum_done")
        s_gcol_out = sem("gcol_out")
        s_ug_made = sem("ug_made")
        s_grow_done = sem("grow_done")
        s_egrow_made = sem("egrow_made")
        s_gdist_made = sem("gdist_made")
        s_eg_made = sem("eg_made")
        s_betas_made = sem("betas_made")
        s_beg_made = sem("beg_made")
        s_dmin_made = sem("dmin_made")
        s_dtt_made = sem("dtt_made")
        s_dti_made = sem("dti_made")
        s_k_turned = sem("k_turned")
        s_v_turned = sem("v_turned")
        s_kb_made = sem("kb_made")
        s_kh_made = sem("kh_made")
        s_vb_made = sem("vb_made")
        s_kk_done = sem("kk_done")
        s_lt_made = sem("lt_made")
        s_qk_done = sem("qk_done")
        s_ab_made = sem("ab_made")
        s_x_identity = sem("x_identity")
        s_ltm_made = sem("ltm_made")
        s_p_done = sem("p_done")
        s_p_out = sem("p_out")
        s_dx_done = sem("dx_done")
        s_xi_new = sem("xi_new")
        s_xit_new = sem("xit_new")
        s_qg_made = sem("qg_made")
        s_og_done = sem("og_done")
        s_sg_done = sem("sg_done")
        s_sg_new = sem("sg_new")
        s_wt_done = sem("wt_done")
        s_wt_out = sem("wt_out")
        s_u_done = sem("u_done")
        s_u_out = sem("u_out")
        s_od_done = sem("od_done")
        s_sd_done = sem("sd_done")
        s_sd_scaled = sem("sd_scaled")
        s_sd_new = sem("sd_new")
        s_o_squared = sem("o_squared")
        s_o_summed = sem("o_summed")
        s_o_lned = sem("o_lned")
        s_o_rsed = sem("o_rsed")
        s_o_gated = sem("o_gated")
        s_mix_turned = sem("mix_turned")
        s_mix_out = sem("mix_out")
        s_mix_stored = sem("mix_stored")
        s_st_loaded = sem("st_loaded")
        s_masked_qk = sem("masked_qk")
        s_masked_w = sem("masked_w")
        s_masked_k = sem("masked_k")
        s_sg_scaled = sem("sg_scaled")
        s_states_stored = sem("states_stored")
        s_conv_stored = sem("conv_stored")
        s_at_cleared = sem("at_cleared")
        s_hs_cleared = sem("hs_cleared")
        s_held = sem("held")

        block = ctx.enter_context(nc.Block())

        def heads(b):
            return bank[b][:, :].rearrange("p (h i) -> p h i", h=H)

        def halves(b):
            return bank[b][:, 0:2 * C].rearrange("p (g i) -> p g i", g=2)

        @block.sync
        def _(sp):
            sp.dma_start(xt[:, :], x_prompt[0:C, :]).then_inc(s_x_loaded, 16)
            for dst, src in ((g1[:, :], norm1_g.rearrange("(k p) -> p k", p=C)), (wa2[:, :], w_a2),
                             (ba[:, :], b_a.rearrange("(k p) -> p k", p=C)),
                             (gains[:, 0, :], gla_g.partition_broadcast(C)),
                             (gains[:, 1, :], gdn_g.partition_broadcast(C)),
                             (alog[:, :], a_log.partition_broadcast(C)),
                             (dtb[:, :], dt_bias.partition_broadcast(C))):
                sp.dma_start(dst, src, allow_slow_non_contiguous=True).then_inc(s_consts_loaded, 16)
            for p in range(3):
                cols = slice(p * 512, p * 512 + 512)
                stage = osq[p % 2][:, :, :].rearrange("p h v -> p (h v)")
                if p == 2:
                    sp.wait_ge(s_cw_turned, 1)
                sp.dma_start(stage[0:4, :], conv_w[:, cols]).then_inc(s_taps_loaded, 16)
                sp.dma_start(stage[4:28, :], state_conv[:, cols]).then_inc(s_taps_loaded, 16)
            for k in range(KT):
                sp.dma_start(w[:, k, :], w_in[k * C:(k + 1) * C, :]).then_inc(s_w_loaded, 16)
            out = mix_t.rearrange("(k p) n -> p k n", p=C)
            sp.wait_ge(s_x_normed, 1)
            sp.dma_start(xt[:, :], x_prompt[C:2 * C, :]).then_inc(s_x_loaded, 16)
            with sp.Fori(0, TILES - 2) as t:
                n = sp.snap(t + 1)
                m = sp.snap(t + 2)
                sp.wait_ge(s_x_normed, m)
                sp.dma_start(xt[:, :], x_prompt[bass.ds(m * C, C), :]).then_inc(s_x_loaded, 16)
                sp.wait_ge(s_mix_out, n * 2)
                sp.dma_start(out[:, :, bass.ds(t * C, C)], mixt[:, :, :]).then_inc(s_mix_stored, 16)
            sp.wait_ge(s_x_normed, TILES)
            sp.dma_start(xt[0:S, :], x_sample).then_inc(s_x_loaded, 16)
            sp.wait_ge(s_mix_out, (TILES - 1) * 2)
            sp.dma_start(out[:, :, T - 2 * C:T - C], mixt[:, :, :]).then_inc(s_mix_stored, 16)
            sp.wait_ge(s_proj_out, GROUPS * TILES)
            sp.dma_start(conv_p, proj[C - 3:C, O_QKV:O_QKV + QKV]).then_inc(s_conv_stored, 16)
            sp.wait_ge(s_mix_out, TILES * 2)
            sp.dma_start(out[:, :, T - C:T], mixt[:, :, :]).then_inc(s_mix_stored, 16)
            sp.wait_ge(s_proj_out, GROUPS * (TILES + 1))
            for b in range(NB):
                sp.dma_start(conv_s[b], proj[b * TS + 1:b * TS + TS, O_QKV:O_QKV + QKV])\
                    .then_inc(s_conv_stored, 16)
            sp.wait_ge(s_sg_new, TILES)
            sp.wait_ge(s_sd_new, TILES)
            rows_of = [slice(64 * (h % 2), 64 * (h % 2) + 64) for h in range(H)]
            for h in range(H):
                sp.dma_start(gla_p[h], hgla[rows_of[h], h, :]).then_inc(s_states_stored, 16)
            sp.dma_start(gdn_p, hgdn[:, :, :]).then_inc(s_states_stored, 16)
            sp.wait_ge(s_hs_cleared, 1)
            for h in range(H):
                sp.dma_start(hs_gla[rows_of[h], h, :, :], state_gla[h]).then_inc(s_st_loaded, 16)
            for h in range(H):
                sp.dma_start(hs_gdn[:, h, :, :], state_gdn[h]).then_inc(s_st_loaded, 16)
            sp.wait_ge(s_mix_out, 2 * (TILES + 1))
            sp.dma_start(out[:, :, T:T + S], mixt[:, :, 0:S]).then_inc(s_mix_stored, 16)
            sp.wait_ge(s_sg_new, TILES + 2 * H)
            sp.wait_ge(s_sd_new, TILES + 2 * H)
            for h in range(H):
                sp.dma_start(gla_s[h], hs_gla[rows_of[h], h, :, :]).then_inc(s_states_stored, 16)
            for h in range(H):
                sp.dma_start(gdn_s[h], hs_gdn[:, h, :, :]).then_inc(s_states_stored, 16)
            sp.wait_ge(s_mix_stored, 16 * (TILES + 1))
            sp.wait_ge(s_states_stored, 16 * (H + 1 + 2 * H))
            sp.wait_ge(s_conv_stored, 16 * (NB + 1))

        @block.gpsimd
        def _(gp):
            gp.memset(ident[:, :], 0.0)
            gp.memset(incl[:, :], 1.0)
            gp.memset(seq_s[:, :], 1.0)
            gp.memset(cols_s[:, :, :], 1.0)
            gp.memset(rows_s[:, :], 1.0)
            gp.memset(reset_s[:, :], 1.0)
            gp.memset(level[:, :, :], 0.0).then_inc(s_masks_made, 1)
            gp.wait_ge(s_masks_made, 1)
            gp.memset(reset_s[:, :].rearrange("p (b i) -> p b i", b=NB)[:, :, 0], 0.0)
            gp.affine_select(out=ident[:, :], in_=ident[:, :], compare_op=ALU.not_equal, fill=1.0, base=0,
                             pattern=[[-1, C]], channel_multiplier=1)
            gp.affine_select(out=incl[:, :], in_=incl[:, :], compare_op=ALU.is_ge, fill=0.0, base=0,
                             pattern=[[1, C]], channel_multiplier=-1)
            for l, span in enumerate(SPANS):
                v = level[:, l, :].rearrange("p (b r i) -> p b r i", r=2, i=span)[:, :, 1, :]
                x = gp.memset(v, 1.0)
            x.then_inc(s_masks_made, 1)
            gp.wait_ge(s_masks_made, 2)

            def within(v, pattern, row, length, low):
                steps = pattern if low else [[-p, n] for p, n in pattern]
                return gp.affine_select(out=v, in_=v, compare_op=ALU.is_ge, fill=0.0,
                                        base=0 if low else length - 1, pattern=steps,
                                        channel_multiplier=row if low else -row)
            for low in (True, False):
                within(seq_s[:, :].rearrange("p (b i) -> p b i", b=NB), [[-TS, NB], [0, TS]], 1, TS, low)
                within(cols_s[:, :, :], [[-TS, NB], [1, S]], 0, TS, low)
                within(rows_s[:, :], [[-TS, NB]], 1, TS, low)
                for l, span in enumerate(SPANS):
                    v = level[:, l, :].rearrange("p (b r i) -> p b r i", r=2, i=span)[:, :, 1, :]
                    x = within(v, [[-2 * span, C // (2 * span)], [0, span]], 1, span, low)
                x.then_inc(s_masks_made, 1)
                gp.wait_ge(s_masks_made, 4 - low)
            la_, lb_ = SAMPLE_LEVELS
            gp.tensor_tensor(incl_s[:, :], ident[0:S, 0:S], level[0:S, la_, 0:S], ALU.add)\
                .then_inc(s_masks_made, 1)
            gp.wait_ge(s_masks_made, 5)
            gp.tensor_tensor(incl_s[:, :], incl_s[:, :], level[0:S, lb_, 0:S], ALU.add)\
                .then_inc(s_masks_made, 1)
            gp.wait_ge(s_consts_loaded, 7 * 16)
            gp.tensor_scalar(gains[:, :, :], gains[:, :, :], 0.5, None, ALU.mult).then_inc(s_masks_made, 1)

            def mixer(t, n, sample):
                N = S if sample else C
                levels = SAMPLE_LEVELS if sample else range(NL)
                gp.wait_ge(s_proj_out, n * GROUPS)
                gp.wait_ge(s_og_done, t)
                gp.wait_ge(s_sg_done, t)
                gp.sem_inc(s_held, 1)
                gp.tensor_copy(va[0:N, :, :], proj[0:N, O_VA:O_VA + H * DV]
                               .rearrange("p (h v) -> p h v", h=H)).then_inc(s_va_copied, 1)
                gp.wait_ge(s_gates_silu, n * 2)
                gp.wait_ge(s_masks_made, 7)
                for g in range(2):
                    x = gp.tensor_tensor(gate[0:N, g, :, :], gate[0:N, g, :, :],
                                         gains[0:N, g, :].unsqueeze(1).to_broadcast([N, H, DV]), ALU.mult)
                x.then_inc(s_gates_made, 1)
                gp.wait_ge(s_g_made, n)
                gp.wait_ge(s_grow_done, t)
                m = incl_s if sample else incl
                gp.tensor_tensor(ug[0:N, :, 0:N], m[0:N, 0:N].unsqueeze(1).to_broadcast([N, H, N]),
                                 gg[0:N, :].unsqueeze(2).to_broadcast([N, H, N]), ALU.mult)\
                    .then_inc(s_ug_made, 1)
                half = (len(levels) + 1) // 2
                gp.wait_ge(s_qe_made, 2 * t + 1)
                for l in list(levels)[:half]:
                    x = gp.tensor_tensor(ke[:, l, :, 0:N], qka[:, 2:4, 0:N], ex[:, l, :, 0:N], ALU.mult)
                x.then_inc(s_ke_made, 1)
                gp.wait_ge(s_qe_made, 2 * n)
                for l in list(levels)[half:]:
                    gp.tensor_tensor(ke[:, l, :, 0:N], qka[:, 2:4, 0:N], ex[:, l, :, 0:N], ALU.mult)
                gp.tensor_tensor(kl[:, :, 0:N], qka[:, 2:4, 0:N], ex[:, E_LAST, :, 0:N], ALU.mult)\
                    .then_inc(s_ke_made, 1)
                gp.wait_ge(s_at_done, ROUNDS * t + (len(levels) + 2) // 2)
                gp.sem_inc(s_held, 1)
                gp.tensor_copy(xi[0:N, :, 0:N], ident[0:N, 0:N].unsqueeze(1).to_broadcast([N, H, N]))
                gp.tensor_copy(xit[0:N, :, 0:N], ident[0:N, 0:N].unsqueeze(1).to_broadcast([N, H, N]))\
                    .then_inc(s_x_identity, 1)
                inv = list(reversed(levels))
                base = NL * t
                for a, l in enumerate(inv):
                    gp.wait_ge(s_lt_made, n)
                    gp.wait_ge(s_p_done, base + a)
                    gp.tensor_tensor(ltm[0:N, :, 0:N], lt[0:N, :, 0:N],
                                     level[0:N, l, 0:N].unsqueeze(1).to_broadcast([N, H, N]), ALU.mult)\
                        .then_inc(s_ltm_made, 1)
            mixer(0, 1, False)
            with gp.Fori(1, TILES) as t:
                mixer(t, gp.snap(t + 1), False)
            gp.wait_ge(s_proj_done, GROUPS * (TILES + 1))
            gp.memset(hs_gla[:, :, :, :], 0.0).then_inc(s_hs_cleared, 1)
            mixer(TILES, TILES + 1, True)
            n = TILES + 1
            rows = rows_s[:, :].unsqueeze(2)
            gp.wait_ge(s_proj_done, GROUPS * n)
            gp.wait_ge(s_ked_out, n)
            for b in range(NB):
                x = gp.tensor_scalar(mk_gla[0:S, b, :], ked[0:S, :], rows_s[:, b:b + 1], None, ALU.mult)
            x.then_inc(s_masked_k, 1)
            gp.wait_ge(s_kh_made, n)
            for b in range(NB):
                x = gp.tensor_scalar(mk_gdn[0:S, b, :, :], kh[0:S, :, :], rows_s[:, b:b + 1], None, ALU.mult)
            x.then_inc(s_masked_k, 1)

        @block.tensor
        def _(pe):
            def front_turn(m, N):
                pe.wait_ge(s_x_normed, m)
                pe.wait_ge(s_proj_out, GROUPS * (m - 1))
                for k in range(KT):
                    x = pe.transpose(heads(k // 4)[:, k % 4, 0:N], xn[0:N, k * C:(k + 1) * C],
                                     ident[0:N, 0:N])
                x.then_inc(s_hn_turned, 1)

            def project(m, part, N):
                g, quarter = divmod(part, 4)
                if part == 0:
                    pe.wait_ge(s_hn_out, m)
                elif quarter == 0:
                    pe.wait_ge(s_proj_out, GROUPS * (m - 1) + g - 1)
                for k in range(quarter * KT // 4, (quarter + 1) * KT // 4):
                    x = pe.matmul(bank[g % 2][0:N, 0:GW], hnt[:, k, 0:N], w[:, k, g * GW:(g + 1) * GW],
                                  start=(k == 0), stop=(k == KT - 1))
                if quarter == 3:
                    x.then_inc(s_proj_done, 1)

            def mixer(t, n, sample, fill, front):
                N = S if sample else C
                levels = list(SAMPLE_LEVELS if sample else range(NL))
                pe.wait_ge(s_proj_out, n * GROUPS)
                pe.wait_ge(s_p_out, NL * t)
                pe.wait_ge(s_u_out, t)
                for g in range(4):
                    x = pe.transpose(heads(2)[:, g, 0:N], proj[0:N, g * C:(g + 1) * C], ident[0:N, 0:N])
                x.then_inc(s_turned, 1)
                pe.wait_ge(s_o_gated, 2 * t)
                pe.transpose(bank[6][0:RANK, 0:N], proj[0:N, O_LOW:O_LOW + RANK], ident[0:N, 0:N])\
                    .then_inc(s_turned, 1)
                pe.wait_ge(s_sd_new, t)
                pe.wait_ge(s_mix_out, 2 * t)
                for p in range(3):
                    for g in range(4):
                        c0 = O_QKV + (4 * p + g) * C
                        x = pe.transpose(heads(3 + p)[:, g, 0:N], proj[0:N, c0:c0 + C], ident[0:N, 0:N])
                    x.then_inc(s_turned, 1)
                pe.wait_ge(s_low_out, n)
                for g in range(2):
                    x = pe.matmul(halves(7)[:, g, 0:N], wa2[:, g * C:(g + 1) * C], lowt[:, 0:N],
                                  start=True, stop=True)
                x.then_inc(s_a_done, 1)
                fill(0, 4)
                pe.wait_ge(s_g_made, n)
                pe.matmul(bank[6][0:N, 128:128 + H], (incl_s if sample else incl)[0:N, 0:N], gg[0:N, :],
                          start=True, stop=True)
                pe.matmul(bank[6][0:N, 132:132 + H], (seq_s if sample else ones)[0:N, 0:N], gg[0:N, :],
                          start=True, stop=True).then_inc(s_gcum_done, 1)
                fill(4, 6)
                pe.wait_ge(s_ug_made, n)
                pe.wait_ge(s_qka_out, n)
                if sample:
                    for h in range(H):
                        x = pe.matmul(heads(2)[:, h, 0:N], ones[0:N, :], ug[0:N, h, 0:N],
                                      start=True, stop=True)
                else:
                    x = pe.matmul(bank[2][:, :], ones[:, :], ug[:, :, :].rearrange("p h i -> p (h i)"),
                                  start=True, stop=True)
                x.then_inc(s_grow_done, 1)
                fill(6, 14)
                half = (len(levels) + 1) // 2
                pe.wait_ge(s_qe_made, 2 * t + 1)
                pe.wait_ge(s_ke_made, 2 * t + 1)
                pe.wait_ge(s_a_abs, n)
                pe.wait_ge(s_a_min, n)
                for a, l in enumerate(levels + [NL]):
                    if a // 2 * 2 <= half < a // 2 * 2 + 2 and a % 2 == 0 or a == half == 1:
                        pe.wait_ge(s_qe_made, 2 * n)
                        pe.wait_ge(s_ke_made, 2 * n)
                    if a >= 2 and a % 2 == 0:
                        fill(13 + a // 2, 14 + a // 2)
                        pe.wait_ge(s_at_level, (NL + 1) * t + a)
                    for h in range(H):
                        p0 = 64 * (h % 2)
                        lhs = ke[p0:p0 + 64, l, h // 2, 0:N] if l < NL else qka[p0:p0 + 64, 2 + h // 2, 0:N]
                        rhs = qe[p0:p0 + 64, l, h // 2, 0:N] if l < NL else qka[p0:p0 + 64, h // 2, 0:N]
                        x = pe.matmul(heads(5 + 2 * (h % 2))[0:N, 2 * (a % 2) + h // 2, 0:N], lhs, rhs,
                                      start=True, stop=True)
                    if a % 2 or l == NL:
                        x.then_inc(s_at_done, 1)
                pe.wait_ge(s_conv_sq, n)
                for p in range(2):
                    if sample:
                        for h in range(H):
                            x = pe.matmul(heads(3 + p)[:, h, 0:N], ones[:, :], th[:, 4 * p + h, 0:N],
                                          start=True, stop=True)
                    else:
                        x = pe.matmul(bank[3 + p][:, :], ones[:, :],
                                      th[:, 4 * p:4 * p + 4, :].rearrange("p h i -> p (h i)"),
                                      start=True, stop=True)
                x.then_inc(s_sums_done, 1)
                fill(17, 18)
                pe.wait_ge(s_gcol_out, n)
                for g in range(2):
                    x = pe.transpose(bank[6][0:N, 256 + g * C:256 + (g + 1) * C], kl[:, g, 0:N], ident[:, :])
                x.then_inc(s_kl_turned, 1)
                pe.wait_ge(s_norm_ln, n)
                for h in range(H):
                    x = pe.transpose(heads(4)[0:N, h, :], cv[:, 8 + h, 0:N], ident[:, :])
                x.then_inc(s_v_turned, 1)
                def gla_out():
                    pe.wait_ge(s_va_copied, n)
                    pe.wait_ge(s_at_level, (NL + 1) * t + len(levels) + 1)
                    pe.wait_ge(s_ked_out, n)
                    if sample:
                        pe.wait_ge(s_st_loaded, 16 * 2 * H)
                        pe.wait_ge(s_masked_qk, 1)
                    else:
                        pe.wait_ge(s_sg_new, t)
                    for h in range(H):
                        pe.matmul(heads(6)[0:N, h, :], at[0:N, h % 2, h // 2, 0:N], va[0:N, h, :],
                                  start=True, stop=False)
                        if sample:
                            for b in range(NB):
                                x = pe.matmul(heads(6)[0:N, h, :], mq_gla[:, h // 2, b, :], hs_gla[:, h, b, :],
                                              start=False, stop=(b == NB - 1))
                        else:
                            x = pe.matmul(heads(6)[0:N, h, :], q0[:, h // 2, 0:N], hgla[:, h, :],
                                          start=False, stop=True)
                    x.then_inc(s_og_done, 1)
                fill(18, 19)
                if not sample:
                    gla_out()
                fill(19, 21)
                pe.wait_ge(s_qk_normed, n)
                for h in range(H):
                    x = pe.transpose(heads(3)[0:N, h, :], cv[:, 4 + h, 0:N], ident[:, :])
                x.then_inc(s_k_turned, 1)
                for h in range(H):
                    x = pe.matmul(heads(5)[0:N, h, 0:N], cv[:, 4 + h, 0:N], cv[:, 4 + h, 0:N],
                                  start=True, stop=True)
                x.then_inc(s_kk_done, 1)
                for h in range(H):
                    x = pe.matmul(heads(7)[0:N, h, 0:N], cv[:, 4 + h, 0:N], cv[:, h, 0:N],
                                  start=True, stop=True)
                x.then_inc(s_qk_done, 1)
                if sample:
                    gla_out()
                fill(21, 22)
                if not sample:
                    pe.wait_ge(s_ab_made, n)
                    for h in range(H):
                        x = pe.matmul(heads(7)[:, h, :], ked[:, h // 2 * C:h // 2 * C + C], va[:, h, :],
                                      start=True, stop=True)
                    x.then_inc(s_sg_done, 1)
                pe.wait_ge(s_x_identity, n)
                pe.wait_ge(s_kb_made, n)
                pe.wait_ge(s_vb_made, n)
                def turn_mixed(g):
                    pe.wait_ge(s_o_gated, 2 * t + g + 1)
                    if not sample and g == 0:
                        pe.wait_ge(s_sg_new, n)
                    for h in range(H):
                        x = pe.transpose(heads(7 - 2 * g)[:, h, 0:N], osq[g][0:N, h, :], ident[0:N, 0:N])
                    x.then_inc(s_mix_turned, 1)

                for a in range(len(levels)):
                    if a == 5:
                        turn_mixed(0)
                    pe.wait_ge(s_ltm_made, NL * t + a + 1)
                    pe.wait_ge(s_xi_new, (NL - 1) * t + a)
                    for h in range(H):
                        x = pe.matmul(heads(5)[0:N, h, 0:N], ltm[0:N, h, 0:N], xi[0:N, h, 0:N],
                                      start=True, stop=True)
                    x.then_inc(s_p_done, 1)
                    fill(min(22 + 2 * a, PARTS), min(23 + 2 * a, PARTS))
                    pe.wait_ge(s_p_out, NL * t + a + 1)
                    pe.wait_ge(s_xit_new, NL * t + a)
                    if 0 < a < len(levels) - 1:
                        for h in range(H):
                            pe.matmul(heads(3)[0:N, h, 0:N], xit[0:N, h, 0:N], pp[0:N, h, 0:N],
                                      start=True, stop=True)
                    for h in range(H):
                        x = pe.matmul(heads(4)[0:N, h, 0:N], pp[0:N, h, 0:N], xit[0:N, h, 0:N],
                                      start=True, stop=True)
                    x.then_inc(s_dx_done, 1)
                    fill(min(23 + 2 * a, PARTS), min(24 + 2 * a, PARTS))
                if sample:
                    turn_mixed(0)
                inv_done = NL * t + len(levels)
                pe.wait_ge(s_xit_new, inv_done)
                for h in range(H):
                    x = pe.matmul(heads(5)[:, h, 0:N], kb[0:N, h, :], xit[0:N, h, 0:N], start=True, stop=True)
                x.then_inc(s_wt_done, 1)
                pe.wait_ge(s_wt_out, n)
                pe.wait_ge(s_egrow_made, n)
                pe.wait_ge(s_dmin_made, n)
                if sample:
                    pe.wait_ge(s_masked_w, 1)
                else:
                    pe.wait_ge(s_sd_new, t)
                for h in range(H):
                    pe.matmul(heads(2)[0:N, h, :], xit[0:N, h, 0:N], vb[0:N, h, :], start=True, stop=False)
                    if sample:
                        for b in range(NB):
                            x = pe.matmul(heads(2)[0:N, h, :], mw_gdn[:, h, b, :], hs_gdn[:, h, b, :],
                                          start=False, stop=(b == NB - 1))
                    else:
                        x = pe.matmul(heads(2)[0:N, h, :], wt[:, h, 0:N], hgdn[:, h, :],
                                      start=False, stop=True)
                x.then_inc(s_u_done, 1)
                pe.wait_ge(s_xi_new, (NL - 1) * t + len(levels) - 1)
                pe.wait_ge(s_u_out, n)
                pe.wait_ge(s_ab_made, n)
                pe.wait_ge(s_qg_made, n)
                if not sample:
                    for h in range(H):
                        x = pe.matmul(heads(4)[:, h, :], kh[:, h, :], uu[:, h, :], start=True, stop=True)
                    x.then_inc(s_sd_done, 1)
                for h in range(H):
                    if sample:
                        for b in range(NB):
                            pe.matmul(heads(3)[0:N, h, :], mq_gdn[:, h, b, :], hs_gdn[:, h, b, :],
                                      start=(b == 0), stop=False)
                    else:
                        pe.matmul(heads(3)[0:N, h, :], cv[:, h, 0:N], hgdn[:, h, :], start=True, stop=False)
                    x = pe.matmul(heads(3)[0:N, h, :], ab[0:N, h, 0:N], uu[0:N, h, :], start=False, stop=True)
                x.then_inc(s_od_done, 1)
                front()
                turn_mixed(1)
                if sample:
                    pe.wait_ge(s_masked_k, 1)
                    pe.wait_ge(s_sg_scaled, 1)
                    pe.wait_ge(s_o_gated, 2 * n)
                    for h in range(H):
                        for q in range(2):
                            pos = 2 * h + q
                            if pos >= 2:
                                pe.wait_ge(s_sg_new, TILES + pos - 1)
                            for b in range(4):
                                x = pe.matmul(heads(3 + pos % 2)[:, b, :],
                                              mk_gla[0:S, 4 * q + b, h // 2 * C:h // 2 * C + C], va[0:S, h, :],
                                              start=True, stop=True)
                            x.then_inc(s_sg_done, 1)
                    pe.wait_ge(s_masked_k, 2)
                    for h in range(H):
                        for q in range(2):
                            pos = 2 * h + q
                            if pos >= 2:
                                pe.wait_ge(s_sd_new, TILES + pos - 1)
                            for b in range(4):
                                x = pe.matmul(heads(pos % 2)[:, b, :], mk_gdn[0:S, 4 * q + b, h, :],
                                              uu[0:S, h, :], start=True, stop=True)
                            x.then_inc(s_sd_done, 1)

            pe.wait_ge(s_masks_made, 6)
            pe.wait_ge(s_at_cleared, 1)
            for p in range(3):
                stage = osq[p % 2][:, :, :]
                pe.wait_ge(s_taps_loaded, 16 * (6 if p == 2 else 4))
                for g in range(4):
                    x = pe.transpose(heads(5 + p)[:, g, 0:28], stage[0:28, g, :], ident[0:28, 0:28])
                x.then_inc(s_cw_turned, 1)
            pe.wait_ge(s_cw_out, 3)
            front_turn(1, C)
            pe.wait_ge(s_w_loaded, 16 * KT)
            for part in range(PARTS):
                project(1, part, C)
            front_turn(2, C)

            def fills(m):
                def fill(i, j):
                    for part in range(i, j):
                        project(m, part, C)
                return fill
            mixer(0, 1, False, fills(2), lambda: front_turn(3, C))
            with pe.Fori(1, TILES - 1) as t:
                later = pe.snap(t + 3)
                mixer(t, pe.snap(t + 1), False, fills(pe.snap(t + 2)), lambda: front_turn(later, C))
            mixer(TILES - 1, TILES, False, fills(TILES + 1), lambda: None)
            mixer(TILES, TILES + 1, True, lambda i, j: None, lambda: None)

        @block.scalar
        def _(act):
            def front_norm(m, N, steps):
                if 0 in steps:
                    act.wait_ge(s_x_loaded, 16 * m)
                    act.wait_ge(s_hn_turned, m - 1)
                    act.activation(xn[0:N, :], xt[0:N, :], ACT.Square, accum_out=x_ss[0:N, :])\
                        .then_inc(s_x_squared, 1)
                if 1 in steps:
                    act.wait_ge(s_x_squared, m)
                    act.activation(x_ln[0:N, :], x_ss[0:N, :], ACT.Ln, scale=1.0 / D, bias=eps[0:N, :])\
                        .then_inc(s_x_lned, 1)
                if 2 in steps:
                    act.wait_ge(s_x_lned, m)
                    act.activation(x_rs[0:N, :], x_ln[0:N, :], ACT.Exp, scale=-0.5).then_inc(s_x_rsed, 1)

            def evacuate(m, g, N):
                act.wait_ge(s_proj_done, GROUPS * (m - 1) + g + 1)
                act.copy(proj[0:N, g * GW:(g + 1) * GW], bank[g % 2][0:N, 0:GW]).then_inc(s_proj_out, 1)

            def mixer(t, n, sample, fill, front):
                N = S if sample else C
                levels = list(SAMPLE_LEVELS if sample else range(NL))
                act.wait_ge(s_turned, 5 * t + 2)
                act.wait_ge(s_a_done, t)
                act.copy(lowt[:, 0:N], bank[6][0:RANK, 0:N]).then_inc(s_low_out, 1)
                act.wait_ge(s_halo_kept, t + 1)
                for p in range(3):
                    act.wait_ge(s_turned, 5 * t + 3 + p)
                    if sample:
                        for g in range(4):
                            x = act.copy(cx[:, 4 * p + g, 0:NB * 7].rearrange("p (b i) -> p b i", b=NB)[:, :, 3:7],
                                         heads(3 + p)[:, g, 0:S].rearrange("p (b i) -> p b i", b=NB))
                    else:
                        x = act.copy(cx[:, 4 * p:4 * p + 4, 3:3 + C], heads(3 + p))
                    x.then_inc(s_cx_out, 1)
                act.wait_ge(s_a_done, n)
                act.wait_ge(s_la_made, t)
                act.wait_ge(s_mix_stored, 16 * t)
                for g in range(2):
                    x = act.activation(la_abs[:, g, 0:N], halves(7)[:, g, 0:N], ACT.Abs, bias=ba[:, g:g + 1])
                x.then_inc(s_a_abs, 1)
                act.wait_ge(s_d_abs, n)
                act.wait_ge(s_d_sum, t)
                act.activation(dexp[0:N, :], dabs[0:N, :], ACT.Exp, scale=-1.0).then_inc(s_d_exp, 1)
                act.wait_ge(s_a_abs, n)
                act.activation(la_exp[:, :, 0:N], la_abs[:, :, 0:N], ACT.Exp, scale=-1.0)\
                    .then_inc(s_a_exp, 1)
                act.wait_ge(s_d_exp, n)
                act.activation(dln[0:N, :], dexp[0:N, :], ACT.Ln, bias=one[0:N, :]).then_inc(s_d_ln, 1)
                act.wait_ge(s_a_exp, n)
                act.activation(la_ln[:, :, 0:N], la_exp[:, :, 0:N], ACT.Ln, bias=one[:, :])\
                    .then_inc(s_a_ln, 1)
                act.wait_ge(s_at_done, ROUNDS * t)
                act.wait_ge(s_ke_made, 2 * t)
                act.wait_ge(s_qe_made, 2 * t)
                act.mul(qka[:, 0:2, 0:N], heads(2)[:, 0:2, 0:N], DKA ** -0.5)
                act.copy(qka[:, 2:4, 0:N], heads(2)[:, 2:4, 0:N]).then_inc(s_qka_out, 1)
                act.wait_ge(s_proj_out, n * GROUPS)
                act.wait_ge(s_o_gated, 2 * t)
                for g, c0 in enumerate((O_GA, O_Z)):
                    act.activation(gate[0:N, g, :, :], proj[0:N, c0:c0 + H * DV]
                                   .rearrange("p (h v) -> p h v", h=H), ACT.Tanh, scale=0.5)\
                        .then_inc(s_gates_tanh, 1)
                act.wait_ge(s_betas_made, t)
                act.activation(tbeta[0:N, :], proj[0:N, O_BETA:O_BETA + H], ACT.Tanh, scale=0.5)\
                    .then_inc(s_gates_tanh, 1)
                fill(0)
                act.wait_ge(s_dist_abs, n)
                if sample:
                    for l in levels + [E_LAST, E_ZERO]:
                        x = act.activation(ex[:, l, :, 0:N], ex[:, l, :, 0:N], ACT.Exp, scale=-1.0 / 16)
                else:
                    x = act.activation(ex[:, :, :, :], ex[:, :, :, :], ACT.Exp, scale=-1.0 / 16)
                x.then_inc(s_ex_made, 1)
                act.wait_ge(s_grow_done, n)
                act.wait_ge(s_sd_new, t)
                act.wait_ge(s_qg_made, t)
                act.activation(egrow[:, :, 0:N], heads(2)[:, :, 0:N], ACT.Exp).then_inc(s_egrow_made, 1)
                act.wait_ge(s_gdist_made, n)
                act.wait_ge(s_beg_made, t)
                act.wait_ge(s_kh_made, t)
                act.activation(gdec[0:N, :], gdist[0:N, :], ACT.Exp)
                act.activation(egcol[0:N, :], gcol[0:N, :], ACT.Exp).then_inc(s_eg_made, 1)
                fill(1)
                act.wait_ge(s_tap, 4 * n)
                act.wait_ge(s_mix_turned, 2 * t)
                act.activation(th[:, :, 0:N], cv[:, :, 0:N], ACT.Tanh, scale=0.5).then_inc(s_conv_tanh, 1)
                fill(2)
                act.wait_ge(s_conv_silu, n)
                act.activation(th[:, 0:8, 0:N], cv[:, 0:8, 0:N], ACT.Square).then_inc(s_conv_sq, 1)
                act.wait_ge(s_dmin_made, n)
                act.activation(dtt[0:N, :, 0:N], dtt[0:N, :, 0:N], ACT.Exp).then_inc(s_dtt_made, 1)
                act.wait_ge(s_sums_done, n)
                for p in range(2):
                    x = act.activation(th[:, 4 * p:4 * p + 4, 0:N], heads(3 + p)[:, :, 0:N], ACT.Ln,
                                       bias=eps4[:, :])
                x.then_inc(s_norm_ln, 1)
                act.wait_ge(s_norm_ln, n)
                act.activation(th[:, 0:4, 0:N], th[:, 0:4, 0:N], ACT.Exp, scale=-0.5, bias=lnq[:, :])
                act.activation(th[:, 4:8, 0:N], th[:, 4:8, 0:N], ACT.Exp, scale=-0.5)\
                    .then_inc(s_norm_rs, 1)
                act.wait_ge(s_kl_turned, n)
                if not sample:
                    act.wait_ge(s_sg_done, t)
                act.copy(ked[0:N, :], bank[6][0:N, 256:512]).then_inc(s_ked_out, 1)
                fill(3)
                def inverse_rms(g, front):
                    act.wait_ge(s_o_summed, 2 * t + g + 1)
                    act.activation(o_lnm[0:N, g, :], o_ss[0:N, g, :], ACT.Ln, scale=1.0 / DV, bias=eps[0:N, :])\
                        .then_inc(s_o_lned, 1)
                    if front:
                        front(1)
                    act.wait_ge(s_o_lned, 2 * t + g + 1)
                    act.activation(o_rs[0:N, g, :], o_lnm[0:N, g, :], ACT.Exp, scale=-0.5)\
                        .then_inc(s_o_rsed, 1)
                    if front:
                        front(2)
                act.wait_ge(s_og_done, n)
                act.wait_ge(s_mix_turned, 2 * t)
                act.activation(osq[0][0:N, :, :], heads(6)[0:N, :, :], ACT.Square).then_inc(s_o_squared, 1)
                fill(4)
                front(0)
                inverse_rms(0, front)
                for g in range(5, GROUPS):
                    fill(g)
                act.wait_ge(s_wt_done, n)
                act.wait_ge(s_u_done, t)
                act.mul(wt[:, :, 0:N], heads(5)[:, :, 0:N], -1.0).then_inc(s_wt_out, 1)
                act.wait_ge(s_u_done, n)
                act.wait_ge(s_od_done, t)
                act.copy(uu[0:N, :, :], heads(2)[0:N, :, :]).then_inc(s_u_out, 1)
                act.activation(spare[0:N, :], one[0:N, :], ACT.Ln)
                act.wait_ge(s_od_done, n)
                act.activation(osq[1][0:N, :, :], heads(3)[0:N, :, :], ACT.Square).then_inc(s_o_squared, 1)
                inverse_rms(1, None)
                for g in range(2):
                    act.wait_ge(s_mix_turned, 2 * t + g + 1)
                    act.copy(mixt[:, 4 * g:4 * g + 4, 0:N], heads(7 - 2 * g)[:, :, 0:N])\
                        .then_inc(s_mix_out, 1)

            act.wait_ge(s_consts_loaded, 7 * 16)
            act.activation(expa[:, :], alog[:, :], ACT.Exp).then_inc(s_expa_made, 1)
            for p in range(3):
                act.wait_ge(s_cw_turned, p + 1)
                act.copy(cw[:, 4 * p:4 * p + 4, :], heads(5 + p)[:, :, 0:28]).then_inc(s_cw_out, 1)
            front_norm(1, C, range(3))
            for g in range(GROUPS):
                evacuate(1, g, C)

            front_norm(2, C, range(3))

            def fills(n, m):
                def fill(g):
                    if g == 0:
                        act.wait_ge(s_turned, 5 * n)
                        act.wait_ge(s_va_copied, n)
                        act.wait_ge(s_d_rel, n)
                        act.wait_ge(s_gates_silu, 2 * n)
                        act.wait_ge(s_gates_tanh, 3 * n)
                    evacuate(m, g, C)
                return fill

            def last_fill(g):
                if g == 0:
                    act.wait_ge(s_conv_stored, 16)
                fills(TILES, TILES + 1)(g)
            mixer(0, 1, False, fills(1, 2), lambda step: front_norm(3, C, (step,)))
            with act.Fori(1, TILES - 1) as t:
                n = act.snap(t + 1)
                later = act.snap(t + 3)
                mixer(t, n, False, fills(n, act.snap(t + 2)), lambda step: front_norm(later, C, (step,)))
            mixer(TILES - 1, TILES, False, last_fill, lambda step: None)
            mixer(TILES, TILES + 1, True, lambda g: None, lambda step: None)

        @block.vector
        def _(dve):
            def front_norm(m, N):
                dve.wait_ge(s_x_rsed, m)
                dve.tensor_scalar(xn[0:N, :], xt[0:N, :], x_rs[0:N, :], None, ALU.mult)\
                    .then_inc(s_x_normed, 1)

            def front_out(m, N):
                dve.wait_ge(s_hn_turned, m)
                dve.wait_ge(s_proj_done, GROUPS * (m - 1))
                for b in range(2):
                    x = dve.tensor_tensor(hnt[:, 4 * b:4 * b + 4, 0:N], heads(b)[:, :, 0:N],
                                          g1[:, 4 * b:4 * b + 4].unsqueeze(2).to_broadcast([C, 4, N]), ALU.mult)
                x.then_inc(s_hn_out, 1)

            def mixer(t, n, sample, front):
                N = S if sample else C
                levels = list(SAMPLE_LEVELS if sample else range(NL))
                dve.wait_ge(s_g_made, t)
                dve.wait_ge(s_d_exp, t)
                dve.tensor_tensor(drel[0:N, :], proj[0:N, O_DEC:O_DEC + H], dtb[0:N, :], ALU.add)\
                    .then_inc(s_d_rel, 1)
                dve.wait_ge(s_d_rel, n)
                dve.tensor_scalar(dabs[0:N, :].bitcast(I32), drel[0:N, :].bitcast(I32), ABS_BITS, None,
                                  ALU.bitwise_and).then_inc(s_d_abs, 1)
                dve.wait_ge(s_cx_out, 3 * n)
                dve.wait_ge(s_halo_kept, n + 1 if sample else n)
                dve.wait_ge(s_mix_turned, 2 * t)
                for tap in (0, 1):
                    if tap:
                        dve.wait_ge(s_tap, 4 * t + tap)
                    for c in range(CT):
                        if sample:
                            src = cx[:, c, 0:NB * 7].rearrange("p (b i) -> p b i", b=NB)[:, :, tap:tap + TS]
                            dst = cv[:, c, 0:S].rearrange("p (b i) -> p b i", b=NB)
                        else:
                            src, dst = cx[:, c, tap:tap + C], cv[:, c, :]
                        if tap == 0:
                            x = dve.tensor_scalar(dst, src, cw[:, c, 0:1], None, ALU.mult)
                        else:
                            x = dve.scalar_tensor_tensor(out=dst, in0=src, scalar=cw[:, c, tap:tap + 1],
                                                         in1=dst, op0=ALU.mult, op1=ALU.add)
                    x.then_inc(s_tap, 1)
                for g, c0 in enumerate((O_GA, O_Z)):
                    dve.wait_ge(s_gates_tanh, 3 * t + g + 1)
                    dve.scalar_tensor_tensor(out=gate[0:N, g, :, :].rearrange("p h v -> p (h v)"),
                                             in0=gate[0:N, g, :, :].rearrange("p h v -> p (h v)"), scalar=1.0,
                                             in1=proj[0:N, c0:c0 + H * DV], op0=ALU.add, op1=ALU.mult)\
                        .then_inc(s_gates_silu, 1)
                dve.wait_ge(s_d_ln, n)
                dve.scalar_tensor_tensor(out=drel[0:N, :], in0=drel[0:N, :], scalar=0.0, in1=dln[0:N, :],
                                         op0=ALU.max, op1=ALU.add).then_inc(s_d_sum, 1)
                dve.wait_ge(s_d_sum, n)
                dve.wait_ge(s_expa_made, 1)
                dve.wait_ge(s_ug_made, t)
                dve.wait_ge(s_gcum_done, t)
                dve.scalar_tensor_tensor(out=gg[0:N, :], in0=drel[0:N, :], scalar=-1.0, in1=expa[0:N, :],
                                         op0=ALU.mult, op1=ALU.mult).then_inc(s_g_made, 1)
                dve.wait_ge(s_a_abs, n)
                for g in range(2):
                    x = dve.tensor_scalar(la_min[:, g, 0:N], halves(7)[:, g, 0:N], ba[:, g:g + 1], 0.0,
                                          ALU.add, ALU.min)
                x.then_inc(s_a_min, 1)
                dve.wait_ge(s_a_min, n)
                dve.wait_ge(s_a_ln, n)
                dve.tensor_tensor(la[:, :, 0:N], la_min[:, :, 0:N], la_ln[:, :, 0:N], ALU.subtract)\
                    .then_inc(s_la_made, 1)
                dve.wait_ge(s_la_made, n)
                for g in range(2):
                    x = dve.tensor_tensor_scan(bcum[:, g, 0:N], reset_s[:, :] if sample else ones[:, :],
                                               la[:, g, 0:N], 0.0, ALU.mult, ALU.add)
                x.then_inc(s_b_made, 1)
                dve.wait_ge(s_b_made, n)
                dve.wait_ge(s_ke_made, 2 * t)
                for l in levels + [E_LAST]:
                    span = SPANS[l] if l < NL else (TS if sample else C)
                    width = 2 * span if l < NL else span
                    for g in range(2):
                        b = bcum[:, g, 0:N].rearrange("p (b i) -> p b i", i=width)
                        dve.tensor_tensor(ex[:, l, g, 0:N].rearrange("p (b i) -> p b i", i=width), b,
                                          b[:, :, span - 1:span].to_broadcast([C, N // width, width]),
                                          ALU.subtract)
                dve.tensor_copy(ex[:, E_ZERO, :, 0:N], bcum[:, :, 0:N]).then_inc(s_dist_made, 1)
                dve.wait_ge(s_dist_made, n)
                if sample:
                    for l in levels + [E_LAST, E_ZERO]:
                        x = dve.tensor_scalar(ex[:, l, :, 0:N].bitcast(I32), ex[:, l, :, 0:N].bitcast(I32),
                                              ABS_BITS, None, ALU.bitwise_and)
                else:
                    x = dve.tensor_scalar(ex[:, :, :, :].bitcast(I32), ex[:, :, :, :].bitcast(I32), ABS_BITS, None,
                                          ALU.bitwise_and)
                x.then_inc(s_dist_abs, 1)
                for tap in (2, 3):
                    if tap:
                        dve.wait_ge(s_tap, 4 * t + tap)
                    for c in range(CT):
                        if sample:
                            src = cx[:, c, 0:NB * 7].rearrange("p (b i) -> p b i", b=NB)[:, :, tap:tap + TS]
                            dst = cv[:, c, 0:S].rearrange("p (b i) -> p b i", b=NB)
                        else:
                            src, dst = cx[:, c, tap:tap + C], cv[:, c, :]
                        if tap == 0:
                            x = dve.tensor_scalar(dst, src, cw[:, c, 0:1], None, ALU.mult)
                        else:
                            x = dve.scalar_tensor_tensor(out=dst, in0=src, scalar=cw[:, c, tap:tap + 1],
                                                         in1=dst, op0=ALU.mult, op1=ALU.add)
                    x.then_inc(s_tap, 1)
                if not sample:
                    dve.tensor_copy(cx[:, :, 0:3], cx[:, :, C:C + 3]).then_inc(s_halo_kept, 1)
                dve.wait_ge(s_gates_tanh, 3 * n)
                dve.wait_ge(s_p_out, NL * t)
                dve.tensor_scalar(nbeta[0:N, :], tbeta[0:N, :], 1.0, -0.5, ALU.add, ALU.mult)
                dve.tensor_scalar(hbeta[0:N, :], tbeta[0:N, :], 1.0, 0.25, ALU.add, ALU.mult)\
                    .then_inc(s_betas_made, 1)
                dve.wait_ge(s_gcum_done, n)
                dve.wait_ge(s_eg_made, t)
                dve.tensor_copy(gcol[0:N, :], bank[6][0:N, 128:132])
                dve.tensor_copy(gend[0:N, :], bank[6][0:N, 132:136]).then_inc(s_gcol_out, 1)
                dve.wait_ge(s_gcol_out, n)
                dve.tensor_tensor(gdist[0:N, :], gend[0:N, :], gcol[0:N, :], ALU.subtract)\
                    .then_inc(s_gdist_made, 1)
                dve.wait_ge(s_ex_made, n)
                dve.wait_ge(s_og_done, t)
                half = (len(levels) + 1) // 2
                for l in levels[:half]:
                    x = dve.tensor_tensor(qe[:, l, :, 0:N], qka[:, 0:2, 0:N], ex[:, l, :, 0:N], ALU.mult)
                x.then_inc(s_qe_made, 1)
                for l in levels[half:]:
                    dve.tensor_tensor(qe[:, l, :, 0:N], qka[:, 0:2, 0:N], ex[:, l, :, 0:N], ALU.mult)
                dve.tensor_tensor(q0[:, :, 0:N], qka[:, 0:2, 0:N], ex[:, E_ZERO, :, 0:N], ALU.mult)\
                    .then_inc(s_qe_made, 1)
                dve.wait_ge(s_conv_tanh, n)
                for p in range(3):
                    x = dve.scalar_tensor_tensor(out=cv[:, 4 * p:4 * p + 4, 0:N],
                                                 in0=th[:, 4 * p:4 * p + 4, 0:N], scalar=1.0,
                                                 in1=cv[:, 4 * p:4 * p + 4, 0:N], op0=ALU.add, op1=ALU.mult)
                x.then_inc(s_conv_silu, 1)
                dve.wait_ge(s_egrow_made, n)
                dve.wait_ge(s_lt_made, t)
                dve.wait_ge(s_dti_made, t)
                for h in range(H):
                    x = dve.tensor_scalar(dtt[0:N, h, 0:N], heads(2)[0:N, h, 0:N], gcol[0:N, h:h + 1], 0.0,
                                          ALU.subtract, ALU.min)
                x.then_inc(s_dmin_made, 1)
                dve.wait_ge(s_eg_made, n)
                dve.wait_ge(s_kb_made, t)
                dve.scalar_tensor_tensor(out=begcol[0:N, :], in0=egcol[0:N, :], scalar=-1.0,
                                         in1=nbeta[0:N, :], op0=ALU.mult, op1=ALU.mult)\
                    .then_inc(s_beg_made, 1)
                dve.wait_ge(s_dtt_made, n)
                dve.wait_ge(s_ab_made, t)
                m_ = (incl_s if sample else incl)[0:N, 0:N]
                dve.tensor_tensor(dti[0:N, :, 0:N], dtt[0:N, :, 0:N],
                                  m_.unsqueeze(1).to_broadcast([N, H, N]), ALU.mult)\
                    .then_inc(s_dti_made, 1)
                if sample:
                    dve.memset(at[0:S, :, :, 0:S], 0.0).then_inc(s_at_cleared, 1)
                    dve.wait_ge(s_at_cleared, 2)
                for a, l in enumerate(levels + [NL]):
                    dve.wait_ge(s_at_done, ROUNDS * t + a // 2 + 1)
                    dve.wait_ge(s_at_level, (NL + 1) * t + a)
                    dve.sem_inc(s_held, 1)
                    msk = (level[0:N, l, 0:N] if l < NL else ident[0:N, 0:N]).bitcast(I32)
                    for e in range(2):
                        x = dve.copy_predicated(at[0:N, e, :, 0:N], msk.unsqueeze(1).to_broadcast([N, 2, N]),
                                                heads(5 + 2 * e)[0:N, 2 * (a % 2):2 * (a % 2) + 2, 0:N])
                    x.then_inc(s_at_level, 1)
                dve.wait_ge(s_norm_rs, n)
                for p in range(2):
                    x = dve.tensor_tensor(cv[:, 4 * p:4 * p + 4, 0:N], cv[:, 4 * p:4 * p + 4, 0:N],
                                          th[:, 4 * p:4 * p + 4, 0:N], ALU.mult)
                x.then_inc(s_qk_normed, 1)
                dve.wait_ge(s_k_turned, n)
                dve.wait_ge(s_beg_made, n)
                dve.wait_ge(s_wt_done, t)
                dve.tensor_tensor(kb[0:N, :, :], heads(3)[0:N, :, :],
                                  begcol[0:N, :].unsqueeze(2).to_broadcast([N, H, DV]), ALU.mult)\
                    .then_inc(s_kb_made, 1)
                if not sample:
                    dve.wait_ge(s_sd_done, t)
                dve.tensor_tensor(kh[0:N, :, :], heads(3)[0:N, :, :],
                                  gdec[0:N, :].unsqueeze(2).to_broadcast([N, H, DV]), ALU.mult)\
                    .then_inc(s_kh_made, 1)
                dve.wait_ge(s_v_turned, n)
                dve.wait_ge(s_betas_made, n)
                dve.tensor_tensor(vb[0:N, :, :], heads(4)[0:N, :, :],
                                  hbeta[0:N, :].unsqueeze(2).to_broadcast([N, H, DV]), ALU.mult)\
                    .then_inc(s_vb_made, 1)
                dve.wait_ge(s_kk_done, n)
                dve.wait_ge(s_ltm_made, NL * t)
                dve.tensor_tensor(lt[0:N, :, 0:N], heads(5)[0:N, :, 0:N], dtt[0:N, :, 0:N], ALU.mult)\
                    .then_inc(s_lt_made, 1)
                dve.wait_ge(s_qk_done, n)
                dve.wait_ge(s_dti_made, n)
                dve.tensor_tensor(ab[0:N, :, 0:N], heads(7)[0:N, :, 0:N], dti[0:N, :, 0:N], ALU.mult)\
                    .then_inc(s_ab_made, 1)
                dve.wait_ge(s_egrow_made, n)
                dve.tensor_tensor(cv[:, 0:4, 0:N], cv[:, 0:4, 0:N], egrow[:, :, 0:N], ALU.mult)\
                    .then_inc(s_qg_made, 1)
                if sample:
                    dve.wait_ge(s_st_loaded, 16 * 2 * H)
                    dve.wait_ge(s_qg_made, n)
                    for g in range(2):
                        dve.tensor_tensor(mq_gla[:, g, :, :], cols_s[:, :, :],
                                          q0[:, g, 0:S].unsqueeze(1).to_broadcast([C, NB, S]), ALU.mult)
                    for h in range(H):
                        x = dve.tensor_tensor(mq_gdn[:, h, :, :], cols_s[:, :, :],
                                              cv[:, h, 0:S].unsqueeze(1).to_broadcast([C, NB, S]), ALU.mult)
                    x.then_inc(s_masked_qk, 1)
                else:
                    dve.wait_ge(s_sg_done, n)
                    for h in range(H):
                        r = slice(64 * (h % 2), 64 * (h % 2) + 64)
                        x = dve.scalar_tensor_tensor(out=hgla[r, h, :], in0=hgla[r, h, :],
                                                     scalar=ex[r, E_ZERO, h // 2, C - 1:C],
                                                     in1=heads(7)[r, h, :], op0=ALU.mult, op1=ALU.add)
                    x.then_inc(s_sg_new, 1)
                dve.wait_ge(s_o_squared, 2 * t + 1)
                dve.tensor_reduce(o_ss[0:N, 0, :], osq[0][0:N, :, :], AX_X, ALU.add).then_inc(s_o_summed, 1)
                def gate_out(g):
                    dve.wait_ge(s_o_rsed, 2 * t + g + 1)
                    dve.wait_ge(s_o_summed, 2 * t + g + 1)
                    dve.wait_ge(s_gates_made, n)
                    for h in range(H):
                        x = dve.scalar_tensor_tensor(out=osq[g][0:N, h, :], in0=heads((6, 3)[g])[0:N, h, :],
                                                     scalar=o_rs[0:N, g, h:h + 1], in1=gate[0:N, g, h, :],
                                                     op0=ALU.mult, op1=ALU.mult)
                    x.then_inc(s_o_gated, 1)

                for a in range(len(levels)):
                    last = a == len(levels) - 1
                    extra = NL - len(levels) if last else 0
                    dve.wait_ge(s_p_done, NL * t + a + 1)
                    if a == 0:
                        dve.wait_ge(s_x_identity, n)
                    dve.wait_ge(s_dx_done, NL * t + a)
                    dve.tensor_tensor(pp[0:N, :, 0:N], heads(5)[0:N, :, 0:N],
                                      nbeta[0:N, :].unsqueeze(2).to_broadcast([N, H, N]), ALU.mult)\
                        .then_inc(s_p_out, 1 + extra)
                    if a == 0:
                        dve.wait_ge(s_p_out, NL * t + 1)
                        dve.tensor_tensor(xi[0:N, :, 0:N], xi[0:N, :, 0:N], pp[0:N, :, 0:N], ALU.add)\
                            .then_inc(s_xi_new, 1)
                    dve.wait_ge(s_dx_done, NL * t + a + 1)
                    if a:
                        dve.wait_ge(s_xi_new, (NL - 1) * t + a)
                        dve.wait_ge(s_xit_new, NL * t + a)
                    if 0 < a and not last:
                        dve.tensor_tensor(xi[0:N, :, 0:N], xi[0:N, :, 0:N], heads(3)[0:N, :, 0:N], ALU.add)\
                            .then_inc(s_xi_new, 1)
                    dve.tensor_tensor(xit[0:N, :, 0:N], xit[0:N, :, 0:N], heads(4)[0:N, :, 0:N], ALU.add)\
                        .then_inc(s_xit_new, 1)
                    if a == min(3, len(levels) - 1):
                        gate_out(0)
                        front[0]()
                if sample:
                    dve.wait_ge(s_wt_out, n)
                    for h in range(H):
                        x = dve.tensor_tensor(mw_gdn[:, h, :, :], cols_s[:, :, :],
                                              wt[:, h, 0:S].unsqueeze(1).to_broadcast([C, NB, S]), ALU.mult)
                    x.then_inc(s_masked_w, 1)
                dve.wait_ge(s_o_squared, 2 * n)
                dve.tensor_reduce(o_ss[0:N, 1, :], osq[1][0:N, :, :], AX_X, ALU.add).then_inc(s_o_summed, 1)
                if not sample:
                    dve.wait_ge(s_od_done, n)
                    dve.tensor_tensor(hgdn[:, :, :], hgdn[:, :, :],
                                      egrow[:, :, C - 1:C].to_broadcast([C, H, DV]), ALU.mult)\
                        .then_inc(s_sd_scaled, 1)
                    dve.wait_ge(s_sd_scaled, n)
                    dve.wait_ge(s_sd_done, n)
                    dve.tensor_tensor(hgdn[:, :, :], hgdn[:, :, :], heads(4), ALU.add)\
                        .then_inc(s_sd_new, 1)
                gate_out(1)
                front[1]()
                if sample:
                    dve.wait_ge(s_og_done, n)
                    for h in range(H):
                        eb = ex[:, E_ZERO, h // 2, 0:S].rearrange("p (b i) -> p b i", b=NB)[:, :, TS - 1:TS]
                        x = dve.tensor_tensor(hs_gla[:, h, :, :], hs_gla[:, h, :, :],
                                              eb.to_broadcast([C, NB, DV]), ALU.mult)
                    x.then_inc(s_sg_scaled, 1)
                    dve.wait_ge(s_od_done, n)
                    for h in range(H):
                        eb = egrow[:, h, 0:S].rearrange("p (b i) -> p b i", b=NB)[:, :, TS - 1:TS]
                        x = dve.tensor_tensor(hs_gdn[:, h, :, :], hs_gdn[:, h, :, :],
                                              eb.to_broadcast([C, NB, DV]), ALU.mult)
                    x.then_inc(s_sd_scaled, 1)
                    dve.wait_ge(s_sg_scaled, 1)
                    dve.wait_ge(s_sd_scaled, n)
                    for pos in range(8):
                        h, q = divmod(pos, 2)
                        r = slice(64 * (h % 2), 64 * (h % 2) + 64)
                        dve.wait_ge(s_sg_done, TILES + pos + 1)
                        dve.tensor_tensor(hs_gla[r, h, 4 * q:4 * q + 4, :], hs_gla[r, h, 4 * q:4 * q + 4, :],
                                          heads(3 + pos % 2)[r], ALU.add).then_inc(s_sg_new, 1)
                    for pos in range(8):
                        h, q = divmod(pos, 2)
                        dve.wait_ge(s_sd_done, TILES + pos + 1)
                        dve.tensor_tensor(hs_gdn[:, h, 4 * q:4 * q + 4, :], hs_gdn[:, h, 4 * q:4 * q + 4, :],
                                          heads(pos % 2), ALU.add).then_inc(s_sd_new, 1)

            dve.wait_ge(s_masks_made, 6)
            for v, x in ((one, 1.0), (eps, EPS), (eps4, 4 * EPS), (lnq, -0.5 * math.log(DV))):
                dve.memset(v[:, :], x)
            dve.memset(ones[:, :], 1.0)
            dve.memset(hgla[:, :, :], 0.0)
            dve.memset(hgdn[:, :, :], 0.0)
            dve.memset(cx[:, :, 0:3], 0.0).then_inc(s_halo_kept, 1)
            dve.memset(at[:, :, :], 0.0).then_inc(s_at_cleared, 1)
            for m in (1, 2):
                front_norm(m, C)
                front_out(m, C)
            mixer(0, 1, False, (lambda: front_norm(3, C), lambda: front_out(3, C)))
            with dve.Fori(1, TILES - 1) as t:
                later = dve.snap(t + 3)
                mixer(t, dve.snap(t + 1), False, (lambda: front_norm(later, C), lambda: front_out(later, C)))
            mixer(TILES - 1, TILES, False, (lambda: None, lambda: None))
            dve.tensor_copy(cx[:, :, 0:NB * 7].rearrange("p c (b i) -> p c b i", b=NB)[:, :, :, 0:3],
                            cw[:, :, 4:28].rearrange("p c (b i) -> p c b i", b=NB))\
                .then_inc(s_halo_kept, 1)
            mixer(TILES, TILES + 1, True, (lambda: None, lambda: None))



def out_projection(nc, x_prompt, x_sample, w_out, norm2_g, ffn_w, state_ffn, mix_t, y, hn, cwt, ident):
    with ExitStack() as ctx:
        def sb(name, shape, dt=F32):
            return ctx.enter_context(nc.sbuf_tensor(name, shape, dt))

        bank = [ctx.enter_context(nc.psum_tensor(f"out_bank{i}", [C, 512], F32)) for i in range(8)]
        wo = sb("wo", [C, KT, D])
        g2 = sb("g2", [C, KT])
        mx = [sb(f"mx{i}", [C, KT, C]) for i in range(2)]
        yn = [sb(f"yn{i}", [C, D]) for i in range(2)]
        sq = sb("sq", [C, D])
        y_ss, y_ln, y_rs = (sb(x, [C, 1]) for x in ("y_ss", "y_ln", "y_rs"))
        eps = sb("eps_out", [C, 1])
        stage = hn[:, :, :].rearrange("p k n -> p (k n)")[0:19, 0:2 * DFF]
        def sem(name):
            return ctx.enter_context(nc.semaphore(name))

        s_wo_loaded = sem("wo_loaded")
        s_x_in = sem("x_in")
        s_cw_staged = sem("cw_staged")
        s_mx_loaded = [sem("mx_loaded0"), sem("mx_loaded1")]
        s_made_ident = sem("made_ident")
        s_made_eps = sem("made_eps")
        s_cw_turned2 = sem("cw_turned2")
        s_cw_kept = sem("cw_kept")
        s_out_done = sem("out_done")
        s_y_new = sem("y_new")
        s_y_sq = sem("y_sq")
        s_y_lned = sem("y_lned")
        s_y_rsed = sem("y_rsed")
        s_y_normed = sem("y_normed")
        s_y_turned = sem("y_turned")
        s_hn_kept = sem("hn_kept")
        block = ctx.enter_context(nc.Block())
        PER = 22

        @block.sync
        def _(sp):
            sp.dma_start(mx[0][:, :, :], mix_t.rearrange("(k p) n -> p k n", p=C)[:, :, 0:C])\
                .then_inc(s_mx_loaded[0], 16)
            for k in range(KT):
                sp.dma_start(wo[:, k, :], w_out[k * C:(k + 1) * C, :]).then_inc(s_wo_loaded, 16)
            sp.wait_ge(s_made_eps, 1)
            sp.dma_start(y[:, 0:TILES, :], x_prompt.rearrange("(t p) d -> p t d", p=C)).then_inc(s_x_in, 16)
            sp.dma_start(y[0:S, TILES, :], x_sample).then_inc(s_x_in, 16)
            sp.dma_start(g2[:, :], norm2_g.rearrange("(k p) -> p k", p=C), allow_slow_non_contiguous=True).then_inc(s_x_in, 16)
            sp.dma_start(stage[0:3, :], ffn_w).then_inc(s_cw_staged, 16)
            sp.dma_start(stage[3:19, :], state_ffn).then_inc(s_cw_staged, 16)
            src = mix_t.rearrange("(k p) n -> p k n", p=C)
            sp.dma_start(mx[1][:, :, :], src[:, :, C:2 * C]).then_inc(s_mx_loaded[1], 16)
            with sp.Fori(0, TILES // 2 - 1) as i:
                n = sp.snap(2 * i)
                sp.wait_ge(s_out_done, n + 1)
                sp.dma_start(mx[0][:, :, :], src[:, :, bass.ds((n + 2) * C, C)]).then_inc(s_mx_loaded[0], 16)
                sp.wait_ge(s_out_done, n + 2)
                sp.dma_start(mx[1][:, :, :], src[:, :, bass.ds((n + 3) * C, C)]).then_inc(s_mx_loaded[1], 16)
            sp.wait_ge(s_out_done, TILES - 1)
            sp.dma_start(mx[0][:, :, 0:S], src[:, :, T:T + S]).then_inc(s_mx_loaded[0], 16)

        @block.gpsimd
        def _(gp):
            gp.memset(ident[:, :], 0.0).then_inc(s_made_ident, 1)
            gp.wait_ge(s_made_ident, 1)
            gp.affine_select(out=ident[:, :], in_=ident[:, :], compare_op=ALU.not_equal, fill=1.0, base=0,
                             pattern=[[-1, C]], channel_multiplier=1).then_inc(s_made_ident, 1)

        @block.tensor
        def _(pe):
            def project(t, p):
                pe.wait_ge(s_mx_loaded[p], 8 * (t - p) + 16)
                if not isinstance(t, int) or t >= 2:
                    pe.wait_ge(s_y_new, 2 * t - 2)
                for e in range(2):
                    for k in range(KT):
                        x = pe.matmul(bank[2 * p + e][:, :], mx[p][:, k, :], wo[:, k, e * 512:e * 512 + 512],
                                      start=(k == 0), stop=(k == KT - 1))
                x.then_inc(s_out_done, 1)

            def turn(t, p):
                pe.wait_ge(s_y_normed, t + 1)
                if not isinstance(t, int) or t >= 2:
                    pe.wait_ge(s_hn_kept, t - 1)
                for k in range(KT):
                    x = pe.transpose(bank[4 + 2 * p + k // 4][:, k % 4 * C:k % 4 * C + C],
                                     yn[p][:, k * C:(k + 1) * C], ident[:, :])
                x.then_inc(s_y_turned, 1)

            pe.wait_ge(s_made_ident, 2)
            pe.wait_ge(s_cw_staged, 32)
            for c in range(2 * FT):
                x = pe.transpose(bank[4 + c // PER][:, c % PER * 19:c % PER * 19 + 19],
                                 stage[:, c * C:(c + 1) * C], ident[0:19, 0:19])
            x.then_inc(s_cw_turned2, 1)
            pe.wait_ge(s_wo_loaded, 16 * KT)
            project(0, 0)
            project(1, 1)
            pe.wait_ge(s_cw_kept, 1)
            turn(0, 0)
            project(2, 0)
            turn(1, 1)
            with pe.Fori(1, TILES // 2) as i:
                n = pe.snap(2 * i)
                project(n + 1, 1)
                turn(n, 0)
                project(n + 2, 0)
                turn(n + 1, 1)
            turn(TILES, 0)

        @block.scalar
        def _(act):
            def norm(n):
                act.wait_ge(s_y_new, 2 * n)
                act.activation(sq[:, :], y[:, bass.ds(n - 1, 1), :].rearrange("p t d -> p (t d)"), ACT.Square,
                               accum_out=y_ss[:, :]).then_inc(s_y_sq, 1)
                act.wait_ge(s_y_sq, n)
                act.activation(y_ln[:, :], y_ss[:, :], ACT.Ln, scale=1.0 / D, bias=eps[:, :])\
                    .then_inc(s_y_lned, 1)
                act.wait_ge(s_y_lned, n)
                act.wait_ge(s_y_normed, n - 1)
                act.activation(y_rs[:, :], y_ln[:, :], ACT.Exp, scale=-0.5).then_inc(s_y_rsed, 1)
            act.wait_ge(s_made_eps, 1)
            act.wait_ge(s_cw_turned2, 1)
            for e in range(2):
                x = act.copy(cwt[:, e * PER:(e + 1) * PER, :],
                             bank[4 + e][:, 0:PER * 19].rearrange("p (c r) -> p c r", r=19))
            x.then_inc(s_cw_kept, 1)
            norm(1)
            with act.Fori(2, YT + 1) as n:
                norm(n)

        @block.vector
        def _(dve):
            def tile(t, p, N):
                dve.wait_ge(s_out_done, t + 1)
                yt = y[:, bass.ds(t, 1), :]
                for e in range(2):
                    v = yt[:, :, e * 512:e * 512 + 512].rearrange("p t d -> p (t d)")
                    dve.tensor_tensor(v, v, bank[2 * p + e][:, :], ALU.add).then_inc(s_y_new, 1)
                dve.wait_ge(s_y_rsed, t + 1)
                if not isinstance(t, int) or t >= 2:
                    dve.wait_ge(s_y_turned, t - 1)
                dve.tensor_scalar(yn[p][:, :], yt.rearrange("p t d -> p (t d)"), y_rs[:, :], None, ALU.mult)\
                    .then_inc(s_y_normed, 1)

            def keep(t, p, N):
                dve.wait_ge(s_y_turned, t + 1)
                for b in range(2):
                    x = dve.tensor_tensor(hn[:, 4 * b:4 * b + 4, bass.ds(t * C, N)],
                                          bank[4 + 2 * p + b][:, :].rearrange("p (k i) -> p k i", k=4)[:, :, 0:N],
                                          g2[:, 4 * b:4 * b + 4].unsqueeze(2).to_broadcast([C, 4, N]), ALU.mult)
                x.then_inc(s_hn_kept, 1)
            dve.memset(eps[:, :], EPS)
            dve.memset(y[:, TILES, :], 0.0).then_inc(s_made_eps, 1)
            dve.wait_ge(s_x_in, 48)
            tile(0, 0, C)
            tile(1, 1, C)
            keep(0, 0, C)
            tile(2, 0, C)
            keep(1, 1, C)
            with dve.Fori(1, TILES // 2) as i:
                n = dve.snap(2 * i)
                tile(n + 1, 1, C)
                keep(n, 0, C)
                tile(n + 2, 0, C)
                keep(n + 1, 1, C)
            keep(TILES, 0, S)


def mlp(nc, w_up, w_down, norm_f_g, y, hn, cwt, ident, y_p, y_s, ffn_p, ffn_s):
    with ExitStack() as ctx:
        def sb(name, shape, dt=F32):
            return ctx.enter_context(nc.sbuf_tensor(name, shape, dt))

        bank = [ctx.enter_context(nc.psum_tensor(f"mlp_bank{i}", [C, 512], F32)) for i in range(8)]
        wu = [sb(f"wu{i}", [C, 2, KT, C]) for i in range(2)]
        wd = sb("wd", [C, D])
        raw = [sb(f"raw{e}", [C, 2 + T]) for e in range(2)]
        raws = [sb(f"raws{e}", [C, NB, 2 + TS]) for e in range(2)]
        cf = [sb(f"cf{i}", [C, 2, 19]) for i in range(2)]
        cv = [sb(f"mcv{e}", [C, UW]) for e in range(2)]
        th = sb("mth", [C, UW])
        act_ = [sb(f"act{i}", [C, ALL]) for i in range(2)]
        tails = sb("tails", [C, 2 + 2 * NB, 2 * FT])
        tailt = sb("tailt", [2 * FT, 2 + 2 * NB, C])
        gf = wu[0][:, 0, :, :].rearrange("p k c -> p (k c)")
        f_ss, f_ln, f_rs = (sb(x, [C, YT]) for x in ("f_ss", "f_ln", "f_rs"))
        eps = sb("eps_mlp", [C, 1])
        def sem(name):
            return ctx.enter_context(nc.semaphore(name))

        s_wu_loaded = [sem("wu_loaded0"), sem("wu_loaded1")]
        s_wd_loaded = sem("wd_loaded")
        s_gf_loaded = sem("gf_loaded")
        s_up_done = sem("up_done")
        s_up_out = sem("up_out")
        s_cf_made = sem("cf_made")
        s_zeros_made = sem("zeros_made")
        s_mtap = sem("mtap")
        s_mtanh = sem("mtanh")
        s_msilu = sem("msilu")
        s_act_made = sem("act_made")
        s_down_done = sem("down_done")
        s_y_added = sem("y_added")
        s_tails_kept = sem("tails_kept")
        s_tails_turned = sem("tails_turned")
        s_tails_out = sem("tails_out")
        s_f_sq = sem("f_sq")
        s_f_rsed = sem("f_rsed")
        s_f_out = sem("f_out")
        s_y_stored = sem("y_stored")
        s_tails_stored = sem("tails_stored")
        s_gp_held_mlp = sem("gp_held_mlp")
        block = ctx.enter_context(nc.Block())
        NG = 2 * UB
        ND = 2 * YT
        LAST = UW - S

        def schedule(engine, up, down):
            up(0, 0)
            up(1, 1)
            down(0, 0)
            with engine.Fori(1, FT // 2) as i:
                f = engine.snap(2 * i)
                up(f, 0)
                down(f - 1, 1)
                up(f + 1, 1)
                down(f, 0)
            down(FT - 1, 1)

        def later(f, k=1):
            return not isinstance(f, int) or f >= k

        @block.sync
        def _(sp):
            def up(f, p):
                if later(f, 2):
                    sp.wait_ge(s_up_done, NG * (f - 1))
                for e in range(2):
                    sp.dma_start(wu[p][:, e, :, :], w_up.rearrange("(k p) n -> p k n", p=C)
                                 [:, :, bass.ds(e * DFF + f * C, C)]).then_inc(s_wu_loaded[p], 16)

            def down(f, p):
                if later(f):
                    sp.wait_ge(s_down_done, ND * f)
                sp.dma_start(wd[:, :], w_down[bass.ds(f * C, C), :]).then_inc(s_wd_loaded, 16)
            schedule(sp, up, down)
            sp.wait_ge(s_up_done, NG * FT)
            sp.dma_start(gf, norm_f_g.partition_broadcast(C)).then_inc(s_gf_loaded, 16)
            sp.wait_ge(s_tails_out, 3)
            for r in range(2):
                sp.dma_start(ffn_p[r].rearrange("(f c) -> f c", c=C), tailt[:, r, :])\
                    .then_inc(s_tails_stored, 16)
            sp.dma_start(ffn_s.rearrange("r (f c) -> f r c", c=C), tailt[:, 2:, :])\
                .then_inc(s_tails_stored, 16)
            with sp.Fori(0, TILES) as t:
                sp.wait_ge(s_f_out, t + 1)
                sp.dma_start(y_p[bass.ds(t * C, C), :], y[:, bass.ds(t, 1), :].rearrange("p t d -> p (t d)"))\
                    .then_inc(s_y_stored, 16)
            sp.wait_ge(s_f_out, YT)
            sp.dma_start(y_s, y[0:S, TILES, :]).then_inc(s_y_stored, 16)
            sp.wait_ge(s_y_stored, 16 * YT)
            sp.wait_ge(s_tails_stored, 16 * 3)

        @block.tensor
        def _(pe):
            def up(f, p):
                pe.wait_ge(s_wu_loaded[p], 16 * (f - p) + 32)
                for u in range(UB):
                    for e in range(2):
                        q = 2 * u + e
                        if q >= 4 or later(f):
                            pe.wait_ge(s_up_out, NG * f + q - 3)
                        for k in range(KT):
                            x = pe.matmul(bank[(q + 2 * p) % 4][:, 0:UW], wu[p][:, e, k, :], hn[:, k, u * UW:(u + 1) * UW],
                                          start=(k == 0), stop=(k == KT - 1))
                        x.then_inc(s_up_done, 1)

            def down(f, p):
                pe.wait_ge(s_act_made, UB * (f + 1))
                pe.wait_ge(s_wd_loaded, 16 * (f + 1))
                for t in range(YT):
                    N = S if t == TILES else C
                    for e in range(2):
                        q = 2 * t + e
                        if q >= 4 or later(f):
                            pe.wait_ge(s_y_added, ND * f + q - 3)
                        pe.matmul(bank[4 + (q + 2 * p) % 4][0:N, :], act_[p][:, t * C:t * C + N],
                                  wd[:, e * 512:e * 512 + 512], start=True, stop=True)\
                            .then_inc(s_down_done, 1)
            schedule(pe, up, down)
            pe.wait_ge(s_tails_kept, FT)
            pe.wait_ge(s_y_added, ND * FT)
            for r in range(2 + 2 * NB):
                b, c = divmod(r, 6)
                if r % 6 == 0:
                    pe.wait_ge(s_up_out, NG * FT)
                x = pe.transpose(bank[b + c // 4 * 4][0:2 * FT, c % 4 * C:c % 4 * C + C], tails[:, r, :],
                                 ident[:, :])
                if c == 5:
                    x.then_inc(s_tails_turned, 1)

        @block.scalar
        def _(act):
            def up(f, p):
                for u in range(UB):
                    for e in range(2):
                        q = 2 * u + e
                        act.wait_ge(s_up_done, NG * f + q + 1)
                        if later(f):
                            act.wait_ge(s_act_made, UB * (f - 1) + min(u + 2, UB))
                            if u == UB - 1:
                                act.wait_ge(s_tails_kept, f)
                        n = LAST if u == UB - 1 else UW
                        x = act.copy(raw[e][:, 2 + u * UW:2 + u * UW + n], bank[(q + 2 * p) % 4][:, 0:n])
                        if u == UB - 1:
                            x = act.copy(raws[e][:, :, 2:2 + TS],
                                         bank[(q + 2 * p) % 4][:, n:UW].rearrange("p (b i) -> p b i", b=NB))
                        x.then_inc(s_up_out, 1)
                    act.wait_ge(s_mtap, 6 * (UB * f + u) + 3)
                    if u or later(f):
                        act.wait_ge(s_act_made, UB * f + u)
                    act.activation(th[:, :], cv[0][:, :], ACT.Tanh, scale=0.5).then_inc(s_mtanh, 1)

            schedule(act, up, lambda f, p: None)
            for r in range(3):
                act.wait_ge(s_tails_turned, r + 1)
                act.copy(tailt[:, 6 * r:6 * r + 4, :],
                         bank[r][0:2 * FT, :].rearrange("p (r c) -> p r c", c=C))
                act.copy(tailt[:, 6 * r + 4:6 * r + 6, :],
                         bank[r + 4][0:2 * FT, 0:2 * C].rearrange("p (r c) -> p r c", c=C))\
                    .then_inc(s_tails_out, 1)
            act.wait_ge(s_y_added, ND * FT)
            for t in range(YT):
                N = S if t == TILES else C
                if t >= 2:
                    act.wait_ge(s_f_sq, t - 1)
                act.activation(act_[t % 2][0:N, 0:D], y[0:N, t, :], ACT.Square, accum_out=f_ss[0:N, t:t + 1])\
                    .then_inc(s_f_sq, 1)
            act.wait_ge(s_f_sq, YT)
            act.activation(f_ln[:, :], f_ss[:, :], ACT.Ln, scale=1.0 / D, bias=eps[:, :]).then_inc(s_f_sq, 1)
            act.wait_ge(s_f_sq, YT + 1)
            act.activation(f_rs[:, :], f_ln[:, :], ACT.Exp, scale=-0.5).then_inc(s_f_rsed, 1)

        @block.gpsimd
        def _(gp):
            def up(f, p):
                if later(f, 2):
                    gp.wait_ge(s_act_made, UB * (f - 1))
                gp.sem_inc(s_gp_held_mlp, 1)
                gp.tensor_copy(cf[p][:, 0:1, :], cwt[:, bass.ds(f, 1), :])
                gp.tensor_copy(cf[p][:, 1:2, :], cwt[:, bass.ds(f + FT, 1), :]).then_inc(s_cf_made, 1)
                gp.wait_ge(s_cf_made, 2 * f + 1)
                if later(f):
                    gp.wait_ge(s_act_made, UB * f)
                gp.sem_inc(s_gp_held_mlp, 1)
                for e in range(2):
                    x = gp.tensor_copy(raws[e][:, :, 0:2], cf[p][:, e, 3:19].rearrange("p (b r) -> p b r", b=NB))
                x.then_inc(s_cf_made, 1)
                gp.wait_ge(s_up_out, NG * (f + 1))
                gp.sem_inc(s_gp_held_mlp, 1)
                for e in range(2):
                    c = slice(e * FT, e * FT + FT)
                    gp.tensor_copy(tails[:, 0:2, c][:, :, bass.ds(f, 1)], raw[e][:, T:T + 2].unsqueeze(2))
                    x = gp.tensor_copy(tails[:, 2:, c][:, :, bass.ds(f, 1)]
                                       .rearrange("p (b r) o -> p b (r o)", b=NB),
                                       raws[e][:, :, TS:TS + 2])
                x.then_inc(s_tails_kept, 1)
            schedule(gp, up, lambda f, p: None)

        @block.vector
        def _(dve):
            def up(f, p):
                dve.wait_ge(s_cf_made, 2 * (f + 1))
                for u in range(UB):
                    last = u == UB - 1
                    n = LAST if last else UW
                    c0 = u * UW
                    for e in range(2):
                        dve.wait_ge(s_up_out, NG * f + 2 * u + e + 1)
                        for tap in range(3):
                            if tap:
                                dve.wait_ge(s_mtap, 6 * (UB * f + u) + 3 * e + tap)
                            elif e == 0 and (u or later(f)):
                                dve.wait_ge(s_act_made, UB * f + u)
                            w = cf[p][:, e, tap:tap + 1]
                            parts = [(cv[e][:, 0:n], raw[e][:, c0 + tap:c0 + tap + n])]
                            if last:
                                parts.append((cv[e][:, n:UW].rearrange("p (b i) -> p b i", b=NB),
                                              raws[e][:, :, tap:tap + TS]))
                            for dst, src in parts:
                                if tap == 0:
                                    x = dve.tensor_scalar(dst, src, w, None, ALU.mult)
                                else:
                                    x = dve.scalar_tensor_tensor(out=dst, in0=src, scalar=w, in1=dst,
                                                                 op0=ALU.mult, op1=ALU.add)
                            x.then_inc(s_mtap, 1)
                    dve.wait_ge(s_mtanh, UB * f + u + 1)
                    dve.scalar_tensor_tensor(out=cv[0][:, :], in0=th[:, :], scalar=1.0, in1=cv[0][:, :],
                                             op0=ALU.add, op1=ALU.mult).then_inc(s_msilu, 1)
                    dve.wait_ge(s_msilu, UB * f + u + 1)
                    dve.wait_ge(s_mtap, 6 * (UB * f + u + 1))
                    if later(f, 2):
                        dve.wait_ge(s_down_done, ND * (f - 1))
                    dve.scalar_tensor_tensor(out=act_[p][:, c0:c0 + UW], in0=cv[0][:, :], scalar=0.5,
                                             in1=cv[1][:, :], op0=ALU.mult, op1=ALU.mult)\
                        .then_inc(s_act_made, 1)

            def down(f, p):
                for t in range(YT):
                    N = S if t == TILES else C
                    for e in range(2):
                        q = 2 * t + e
                        dve.wait_ge(s_down_done, ND * f + q + 1)
                        if q == 0 and later(f):
                            dve.wait_ge(s_y_added, ND * f)
                        v = y[0:N, t, e * 512:e * 512 + 512]
                        dve.tensor_tensor(v, v, bank[4 + (q + 2 * p) % 4][0:N, :], ALU.add).then_inc(s_y_added, 1)
            dve.memset(eps[:, :], EPS)
            dve.memset(f_ss[:, :], 1.0)
            for e in range(2):
                x = dve.memset(raw[e][:, 0:2], 0.0)
            x.then_inc(s_zeros_made, 1)
            dve.wait_ge(s_zeros_made, 1)
            schedule(dve, up, down)
            dve.wait_ge(s_f_rsed, 1)
            dve.wait_ge(s_gf_loaded, 16)
            for t in range(YT):
                N = S if t == TILES else C
                dve.scalar_tensor_tensor(out=y[0:N, t, :], in0=y[0:N, t, :], scalar=f_rs[0:N, t:t + 1],
                                         in1=gf[0:N, :], op0=ALU.mult, op1=ALU.mult).then_inc(s_f_out, 1)


def hybrid_layer(nc, x_prompt, x_sample, state_gla, state_gdn, state_gdn_conv, state_ffn_conv,
                 norm1_g, w_in, gla_w_a2, gla_b_a, gla_norm_g, gdn_conv_w, gdn_a_log, gdn_dt_bias,
                 gdn_norm_g, w_out, norm2_g, w_up, ffn_conv_w, w_down, norm_f_g,
                 y_p, y_s, gla_p, gdn_p, conv_p, ffn_p, gla_s, gdn_s, conv_s, ffn_s):
    mix_t = nc.dram_tensor("mix_t", (D, T + S), F32, kind="Internal").ap()
    xp, xs = x_prompt[0], x_sample.rearrange("b t d -> (b t) d")
    mixers(nc, xp, xs,
           state_gla[0].rearrange("b h k v -> h k b v"),
           state_gdn[0].rearrange("b h k v -> h k b v"),
           state_gdn_conv[0].rearrange("b r c -> (b r) c"),
           norm1_g[0], w_in[0], gla_w_a2[0], gla_b_a[0], gla_norm_g[0], gdn_conv_w[0],
           gdn_a_log[0], gdn_dt_bias[0], gdn_norm_g[0], mix_t,
           gla_p[0, 0],
           gdn_p[0, 0].rearrange("h k v -> k h v"), conv_p[0, 0],
           gla_s[0].rearrange("b h k v -> h k b v"),
           gdn_s[0].rearrange("b h k v -> h k b v"), conv_s[0])
    with ExitStack() as ctx:
        y = ctx.enter_context(nc.sbuf_tensor("y", [C, YT, D], F32))
        hn = ctx.enter_context(nc.sbuf_tensor("hn", [C, KT, ALL], F32))
        cwt = ctx.enter_context(nc.sbuf_tensor("cwt", [C, 2 * FT, 19], F32))
        ident = ctx.enter_context(nc.sbuf_tensor("ident_mlp", [C, C], F32))
        out_projection(nc, xp, xs, w_out[0], norm2_g[0], ffn_conv_w[0],
                       state_ffn_conv[0].rearrange("b r c -> (b r) c"), mix_t, y, hn, cwt, ident)
        mlp(nc, w_up[0], w_down[0], norm_f_g, y, hn, cwt, ident, y_p[0],
            y_s.rearrange("b t d -> (b t) d"), ffn_p[0, 0], ffn_s[0].rearrange("b r c -> (b r) c"))


_INS = ["x_prompt", "x_sample", "state_gla", "state_gdn", "state_gdn_conv", "state_ffn_conv",
        "norm1_g", "w_in", "gla_w_a2", "gla_b_a", "gla_norm_g", "gdn_conv_w", "gdn_a_log",
        "gdn_dt_bias", "gdn_norm_g", "w_out", "norm2_g", "w_up", "ffn_conv_w", "w_down", "norm_f_g"]
_OUTS = [(1, T, D), (NB, TS, D), (1, 1, H, DKA, DV), (1, 1, H, DV, DV), (1, 1, 3, QKV),
         (1, 1, 2, 2 * DFF), (1, NB, H, DKA, DV), (1, NB, H, DV, DV), (1, NB, 3, QKV),
         (1, NB, 2, 2 * DFF)]


def kernel(**inputs):
    import numpy as _np
    import concourse.bacc as _bacc
    from concourse import mybir as _mybir
    from concourse.bass_utils import run_bass_kernel_spmd as _run

    nc = _bacc.Bacc("TRN2", target_bir_lowering=False, num_devices=1)
    arrays, args = {}, []
    for name in _INS:
        a = _np.ascontiguousarray(inputs[name])
        arrays[f"in_{name}_dram"] = a
        args.append(nc.dram_tensor(f"in_{name}_dram", a.shape, _mybir.dt.from_np(a.dtype),
                                   kind="ExternalInput").ap())
    for i, shape in enumerate(_OUTS):
        args.append(nc.dram_tensor(f"out_{i}_dram", shape, F32, kind="ExternalOutput").ap())
    hybrid_layer(nc, *args)
    r = _run(nc, [arrays], core_ids=[0])
    return tuple(r.results[0][f"out_{i}_dram"] for i in range(len(_OUTS)))
```
